# Optimizing a Trainium2 kernel written in Bass

```python
import jax
import jax.numpy as jnp
from jax import lax
import numpy as np

D_MODEL = 1024
BATCH = 1
SEQ = 256
DEPTH = 2

CHUNK = 64
N_MIXERS = 2
RMS_EPS = 1e-6
SWA_WINDOW = 128
SWA_CHUNKS = SWA_WINDOW // CHUNK
A_HEADS = 16
A_KV_HEADS = 4
A_GROUP = A_HEADS // A_KV_HEADS
A_HEAD_DIM = 64
A_Q_DIM = A_HEADS * A_HEAD_DIM
A_KV_DIM = A_KV_HEADS * A_HEAD_DIM
A_QKV_DIM = A_Q_DIM + 2 * A_KV_DIM
B_QK_HEADS = 8
B_V_HEADS = 16
B_HEAD_DIM = 128
B_QK_DIM = B_QK_HEADS * B_HEAD_DIM
B_V_DIM = B_V_HEADS * B_HEAD_DIM
B_CONV_DIM = 2 * B_QK_DIM + B_V_DIM
B_IN_DIM = B_CONV_DIM + B_V_DIM + 2 * B_V_HEADS
CONV_WIDTH = 4
D_FF_DENSE = 2816
N_EXPERTS = 8
TOP_K = 2
D_FF_EXPERT = 3584

kernel_name = 'hybrid_swa_sink_gdn_moe_trunk'

def rmsnorm(x, g):
    xf = x.astype(jnp.float32)
    y = xf * lax.rsqrt(jnp.mean(xf * xf, axis=-1, keepdims=True) + RMS_EPS)
    return (y * g.astype(jnp.float32)).astype(x.dtype)

def l2norm(x):
    return x * lax.rsqrt(jnp.sum(x * x, axis=-1, keepdims=True) + RMS_EPS)

def alibi_slopes():
    return jnp.exp2(-8.0 * jnp.arange(1, A_HEADS + 1, dtype=jnp.float32) / A_HEADS)

def chunk_band(t, nc):
    pad = [(0, 0)] * t.ndim
    parts = []
    for back in range(SWA_CHUNKS - 1, -1, -1):
        pad[1] = (back, 0)
        parts.append(jnp.pad(t, pad)[:, :nc])
    return jnp.concatenate(parts, axis=2)

def swa_sink_attention(h, w_qkv, b_qkv, sinks, w_o):
    bsz, seq, _ = h.shape
    nc = seq // CHUNK
    kb_len = SWA_CHUNKS * CHUNK
    qkv = h @ w_qkv + b_qkv
    q, k, v = jnp.split(qkv, [A_Q_DIM, A_Q_DIM + A_KV_DIM], axis=-1)
    q = q.reshape(bsz, nc, CHUNK, A_KV_HEADS, A_GROUP, A_HEAD_DIM)
    k = k.reshape(bsz, nc, CHUNK, A_KV_HEADS, A_HEAD_DIM)
    v = v.reshape(bsz, nc, CHUNK, A_KV_HEADS, A_HEAD_DIM)
    k_band = chunk_band(k, nc)
    v_band = chunk_band(v, nc)
    scores = jnp.einsum('bnqhgd,bnkhd->bhgnqk', q, k_band).astype(jnp.float32) * (A_HEAD_DIM ** -0.5)
    qi = jnp.arange(CHUNK)[:, None]
    kj = jnp.arange(kb_len)[None, :]
    dist = jnp.abs(qi + (SWA_CHUNKS - 1) * CHUNK - kj).astype(jnp.float32)
    slopes = alibi_slopes().reshape(A_KV_HEADS, A_GROUP, 1, 1, 1)
    scores = scores - slopes * dist
    key_chunk = jnp.arange(nc)[:, None] + kj // CHUNK - (SWA_CHUNKS - 1)
    valid = (key_chunk >= 0)[:, None, :]
    scores = jnp.where(valid, scores, -jnp.inf)
    sink = sinks.astype(jnp.float32).reshape(A_KV_HEADS, A_GROUP, 1, 1, 1)
    m = jnp.maximum(jnp.max(scores, axis=-1, keepdims=True), sink)
    p = jnp.exp(scores - m)
    probs = p / (jnp.sum(p, axis=-1, keepdims=True) + jnp.exp(sink - m))
    out = jnp.einsum('bhgnqk,bnkhd->bnqhgd', probs.astype(v.dtype), v_band)
    return out.reshape(bsz, seq, A_Q_DIM) @ w_o

def causal_depthwise_conv(x, w):
    k_w, ch = w.shape
    return lax.conv_general_dilated(x, w[:, None, :], window_strides=(1,), padding=[(k_w - 1, 0)],
                                    dimension_numbers=('NWC', 'WIO', 'NWC'), feature_group_count=ch)

def chunk_gated_delta_rule(q, k, v, beta, g):
    bsz, seq, nh, dk = q.shape
    dv = v.shape[-1]
    nc = seq // CHUNK

    def to_chunks(t):
        return t.reshape(bsz, nc, CHUNK, nh, -1).transpose(0, 3, 1, 2, 4)

    q, k, v = to_chunks(q), to_chunks(k), to_chunks(v)
    beta = beta.reshape(bsz, nc, CHUNK, nh).transpose(0, 3, 1, 2)
    gc = jnp.cumsum(g.reshape(bsz, nc, CHUNK, nh).transpose(0, 3, 1, 2), axis=-1)
    causal = jnp.tril(jnp.ones((CHUNK, CHUNK), dtype=bool))
    strict = jnp.tril(jnp.ones((CHUNK, CHUNK), dtype=bool), k=-1)
    decay = jnp.exp(jnp.where(causal, gc[..., :, None] - gc[..., None, :], -jnp.inf))
    k_beta = k * beta[..., None]
    a_low = jnp.where(strict, jnp.einsum('bhnid,bhnjd->bhnij', k_beta, k) * decay, 0.0)
    eye = jnp.eye(CHUNK, dtype=q.dtype)
    t_inv = lax.linalg.triangular_solve(eye + a_low, jnp.broadcast_to(eye, a_low.shape),
                                        left_side=True, lower=True, unit_diagonal=True)
    u = t_inv @ (v * beta[..., None])
    w = t_inv @ (k_beta * jnp.exp(gc)[..., None])
    attn_intra = jnp.einsum('bhnid,bhnjd->bhnij', q, k) * decay
    q_dec = q * jnp.exp(gc)[..., None]
    g_last = gc[..., -1]
    k_tail = k * jnp.exp(g_last[..., None] - gc)[..., None]

    def step(state, inp):
        q_n, u_n, w_n, a_n, kt_n, gl_n = inp
        v_new = u_n - w_n @ state
        o_n = q_n @ state + a_n @ v_new
        state = state * jnp.exp(gl_n)[..., None, None] + jnp.swapaxes(kt_n, -1, -2) @ v_new
        return state, o_n

    xs = tuple(jnp.moveaxis(t, 2, 0) for t in (q_dec, u, w, attn_intra, k_tail, g_last))
    state0 = jnp.zeros((bsz, nh, dk, dv), dtype=q.dtype)
    _, o = lax.scan(step, state0, xs)
    return o.transpose(1, 0, 3, 2, 4).reshape(bsz, seq, nh, dv)

def gated_deltanet(h, w_in, conv_w, a_log, dt_bias, norm_g, w_o):
    bsz, seq, _ = h.shape
    proj = h @ w_in
    qkv, z, b, a = jnp.split(proj, [B_CONV_DIM, B_CONV_DIM + B_V_DIM, B_CONV_DIM + B_V_DIM + B_V_HEADS], axis=-1)
    qkv = jax.nn.silu(causal_depthwise_conv(qkv, conv_w)).astype(jnp.float32)
    q, k, v = jnp.split(qkv, [B_QK_DIM, 2 * B_QK_DIM], axis=-1)
    rep = B_V_HEADS // B_QK_HEADS
    q = jnp.repeat(l2norm(q.reshape(bsz, seq, B_QK_HEADS, B_HEAD_DIM)) * (B_HEAD_DIM ** -0.5), rep, axis=2)
    k = jnp.repeat(l2norm(k.reshape(bsz, seq, B_QK_HEADS, B_HEAD_DIM)), rep, axis=2)
    v = v.reshape(bsz, seq, B_V_HEADS, B_HEAD_DIM)
    beta = jax.nn.sigmoid(b.astype(jnp.float32))
    g = -jnp.exp(a_log.astype(jnp.float32)) * jax.nn.softplus(a.astype(jnp.float32) + dt_bias.astype(jnp.float32))
    o = chunk_gated_delta_rule(q, k, v, beta, g)
    o = o * lax.rsqrt(jnp.mean(o * o, axis=-1, keepdims=True) + RMS_EPS) * norm_g.astype(jnp.float32)
    o = o * jax.nn.silu(z.astype(jnp.float32).reshape(bsz, seq, B_V_HEADS, B_HEAD_DIM))
    return o.reshape(bsz, seq, B_V_DIM).astype(h.dtype) @ w_o

def swiglu(h, w_gate, w_up, w_down):
    return (jax.nn.silu(h @ w_gate) * (h @ w_up)) @ w_down

def moe_swiglu(h, w_router, w_gate, w_up, w_down):
    bsz, seq, dm = h.shape
    t = h.reshape(-1, dm)
    logits = (t @ w_router).astype(jnp.float32)
    top_v, top_i = lax.top_k(logits, TOP_K)
    gates = jax.nn.softmax(top_v, axis=-1)
    comb = jnp.sum(jax.nn.one_hot(top_i, N_EXPERTS, dtype=jnp.float32) * gates[..., None], axis=1)
    comb = comb.astype(t.dtype)
    out = jnp.zeros_like(t)
    for e in range(N_EXPERTS):
        out = out + comb[:, e:e + 1] * swiglu(t, w_gate[e], w_up[e], w_down[e])
    return out.reshape(bsz, seq, dm)

def setup_inputs(seed: int = 0) -> dict:
    key = jax.random.key(seed)
    ks = jax.random.split(key, 24)
    n_a = (DEPTH + 1) // 2
    n_b = DEPTH // 2
    f32 = jnp.float32

    def w(k, shape, fan_in):
        return jax.random.normal(k, shape, f32) * (fan_in ** -0.5)

    dt = jnp.exp(jax.random.uniform(ks[9], (n_b, B_V_HEADS), f32, np.log(1e-3), np.log(1e-1)))
    return {
        'x': jax.random.normal(ks[0], (BATCH, SEQ, D_MODEL), f32),
        'norm_g': 1.0 + 0.02 * jax.random.normal(ks[1], (DEPTH, 2, D_MODEL), f32),
        'final_norm_g': 1.0 + 0.02 * jax.random.normal(ks[2], (D_MODEL,), f32),
        'attn_w_qkv': w(ks[3], (n_a, D_MODEL, A_QKV_DIM), D_MODEL),
        'attn_b_qkv': 0.02 * jax.random.normal(ks[4], (n_a, A_QKV_DIM), f32),
        'attn_sinks': 0.5 * jax.random.normal(ks[5], (n_a, A_HEADS), f32),
        'attn_w_o': w(ks[6], (n_a, A_Q_DIM, D_MODEL), A_Q_DIM),
        'dn_w_in': w(ks[7], (n_b, D_MODEL, B_IN_DIM), D_MODEL),
        'dn_conv_w': w(ks[8], (n_b, CONV_WIDTH, B_CONV_DIM), CONV_WIDTH),
        'dn_a_log': jnp.log(jax.random.uniform(ks[10], (n_b, B_V_HEADS), f32, 1.0, 16.0)),
        'dn_dt_bias': dt + jnp.log(-jnp.expm1(-dt)),
        'dn_norm_g': 1.0 + 0.02 * jax.random.normal(ks[11], (n_b, B_HEAD_DIM), f32),
        'dn_w_o': w(ks[12], (n_b, B_V_DIM, D_MODEL), B_V_DIM),
        'ffn_w_gate': w(ks[13], (n_a, D_MODEL, D_FF_DENSE), D_MODEL),
        'ffn_w_up': w(ks[14], (n_a, D_MODEL, D_FF_DENSE), D_MODEL),
        'ffn_w_down': w(ks[15], (n_a, D_FF_DENSE, D_MODEL), D_FF_DENSE),
        'moe_w_router': w(ks[16], (n_b, D_MODEL, N_EXPERTS), D_MODEL),
        'moe_w_gate': w(ks[17], (n_b, N_EXPERTS, D_MODEL, D_FF_EXPERT), D_MODEL),
        'moe_w_up': w(ks[18], (n_b, N_EXPERTS, D_MODEL, D_FF_EXPERT), D_MODEL),
        'moe_w_down': w(ks[19], (n_b, N_EXPERTS, D_FF_EXPERT, D_MODEL), D_FF_EXPERT),
    }

def reference(x, norm_g, final_norm_g, attn_w_qkv, attn_b_qkv, attn_sinks, attn_w_o,
              dn_w_in, dn_conv_w, dn_a_log, dn_dt_bias, dn_norm_g, dn_w_o,
              ffn_w_gate, ffn_w_up, ffn_w_down,
              moe_w_router, moe_w_gate, moe_w_up, moe_w_down):
    for i in range(DEPTH):
        j = i // N_MIXERS
        h = rmsnorm(x, norm_g[i, 0])
        if i % N_MIXERS == 0:
            x = x + swa_sink_attention(h, attn_w_qkv[j], attn_b_qkv[j], attn_sinks[j], attn_w_o[j])
        else:
            x = x + gated_deltanet(h, dn_w_in[j], dn_conv_w[j], dn_a_log[j], dn_dt_bias[j], dn_norm_g[j], dn_w_o[j])
        h = rmsnorm(x, norm_g[i, 1])
        f = i // 2
        if i % 2 == 0:
            x = x + swiglu(h, ffn_w_gate[f], ffn_w_up[f], ffn_w_down[f])
        else:
            x = x + moe_swiglu(h, moe_w_router[f], moe_w_gate[f], moe_w_up[f], moe_w_down[f])
    return rmsnorm(x, final_norm_g)


_drawn_inputs = setup_inputs


def setup_inputs(seed=0):
    import zlib

    import numpy as np

    out = dict(_drawn_inputs(seed))
    spreads = {}
    factors = {}
    for name, (base, spread) in spreads.items():
        noise = np.random.default_rng([zlib.crc32(name.encode()), seed]).standard_normal(out[name].shape)
        drawn = base * np.exp(spread * noise) if base else spread * noise
        out[name] = jnp.asarray(drawn.astype(out[name].dtype))
    for name, factor in factors.items():
        out[name] = (out[name] * factor).astype(out[name].dtype)
    return out
```

```python
from contextlib import ExitStack

import numpy as np

import concourse.bass as bass
from concourse import mybir

ALU = mybir.AluOpType
ACT = mybir.ActivationFunctionType
F32 = mybir.dt.float32
F32R = mybir.dt.float32r
I32 = mybir.dt.int32
U32 = mybir.dt.uint32
AX_X = mybir.AxisListType.X

P = 128
SEQ = 256
TB = SEQ // P
D = 1024
KT = D // P
EPS = 1e-6
CHUNK = 64
NCH = SEQ // CHUNK
HEADS, KV_HEADS, HD = 16, 4, 64
QKV = (HEADS + 2 * KV_HEADS) * HD
PAIRS = HEADS // 2
DFF = 2816
QK_DIM, V_DIM, BH = 1024, 2048, 128
VH = 16
GROUPS = 4
GH = VH // GROUPS
IN_DIM = 2 * QK_DIM + 2 * V_DIM + 2 * VH
NE = 8
FFE = 3584
ECH = FFE // 512
BIG = 1e30

PANEL = 2048
RAW, SPLIT = 6, 3

TABLE = {}


def table():
    i, j = np.arange(P)[:, None], np.arange(P)[None, :]
    same = i // CHUNK == j // CHUNK
    parts = {
        "ident": i == j,
        "cum": same & (i <= j),
        "chunk": same,
        "first": (i < CHUNK) & (j >= 0),
        "second": (i >= CHUNK) & (j >= 0),
        "off_strict": np.where(same & (i > j), 0.0, BIG),
        "off_upper": np.where(same & (i <= j), 0.0, BIG),
        "tri": i <= j,
        "ones": (i >= 0) & (j >= 0),
        "iota": j + 0 * i,
    }
    for n in range(6):
        s = 1 << n
        parts[f"level{n}"] = (i // (2 * s) == j // (2 * s)) & (i // s % 2 == 1) & (j // s % 2 == 0)
    at, out = 0, []
    for name, a in parts.items():
        TABLE[name] = at
        at += P
        out.append(a.astype(np.float32))
    return np.ascontiguousarray(np.concatenate(out, axis=1))


def alibi():
    slope = np.exp2(-8.0 * np.arange(1, HEADS + 1, dtype=np.float32) / HEADS)
    dist = np.abs(np.arange(CHUNK)[:, None] + CHUNK - np.arange(2 * CHUNK)[None, :]).astype(np.float32)
    a = -(slope.reshape(PAIRS, 2, 1, 1) * dist).transpose(1, 2, 0, 3).reshape(P, PAIRS, 2 * CHUNK)
    first = a.copy()
    first[:, :, :CHUNK] = -BIG
    return np.ascontiguousarray(np.stack([first, a]).astype(np.float32).reshape(2, P, PAIRS * P))


def trunk(nc, x, norm_g, final_norm_g, w_qkv, b_qkv, sinks, w_o, w_in, conv_w, a_log, dt_bias, dn_norm_g,
          dn_w_o, f_gate, f_up, f_down, w_router, e_gate, e_up, e_down, tab, ali, out):
    sems = {}
    psum = [nc.alloc_psum_tensor(f"bank{n}", [P, 512], F32) for n in range(8)]
    bank = [b[:, :] for b in psum]

    base = (nc.sbuf_base + 63) // 64 * 64
    KB = 1024

    def at(name, n, kb, dt=F32, parts=P):
        return nc.alloc_sbuf_tensor_at(name, [parts, n], dt, offset=base + int(kb * KB))

    raw = at("raw", RAW * PANEL, 0)
    whi = at("whi", SPLIT * PANEL, 48, F32R)
    wlo = at("wlo", SPLIT * PANEL, 72, F32R)
    xhi = at("xhi", 2048, 96, F32R)
    xlo = at("xlo", 2048, 104, F32R)
    X = at("X", TB * D, 112)[:, :].rearrange("p (b d) -> p b d", b=TB)
    tabs = at("tabs", 16 * P, 120)
    par = at("par", 820, 128)
    S = at("S", GH * BH, 131.5)[:, :].rearrange("p (h d) -> p h d", h=GH)
    W0 = 133.5
    gain = at("gain", D, W0)
    H = at("H", TB * D, W0 + 4)[:, :].rearrange("p (b d) -> p b d", b=TB)
    qkv = at("qkv", TB * QKV, W0 + 12)[:, :].rearrange("p (b d) -> p b d", b=TB)
    qT = at("qT", HEADS * SEQ, W0 + 24)[0:HD, :].rearrange("p (n h q) -> p n h q", n=NCH, h=HEADS)
    kT = at("kT", KV_HEADS * (CHUNK + SEQ), W0 + 40)[0:HD, :].rearrange("p (h t) -> p h t", h=KV_HEADS)
    abias = at("abias", 2 * PAIRS * P, W0 + 45)[:, :].rearrange("p (n f) -> p n f", n=2)
    bqkv = at("bqkv", QKV, W0 + 53)
    sc = at("sc", 2 * PAIRS * P, W0 + 59)[:, :].rearrange("p (n f) -> p n f", n=2)
    pT = at("pT", PAIRS * P, W0 + 67)[:, :].rearrange("p (j c) -> p j c", j=PAIRS)
    vsh = at("vsh", 2 * 256, W0 + 71)[:, :].rearrange("p (n f) -> p n f", n=2)
    hhi = at("hhi", 512, W0 + 16, F32R)
    hlo = at("hlo", 512, W0 + 18, F32R)
    sil = at("sil", 512, W0 + 30)
    hid = at("hid", 512, W0 + 32)
    def eight(name, kb):
        return at(name, 8 * P, W0 + kb)[:, :].rearrange("p (n f) -> p n f", n=8)
    kbe, qdec, off0 = eight("kbe", 0), eight("qdec", 4), eight("off0", 8)
    oall = at("oall", TB * V_DIM, W0 + 12)[:, :].rearrange("p (b d) -> p b d", b=TB)
    prj = at("prj", 2 * TB * 512, W0 + 28)[:, :].rearrange("p (n b d) -> p n b d", n=2, b=TB)
    attnT, wT = eight("attnT", 28), eight("wT", 32)
    cv = eight("cv", 36), eight("cv1", 40)
    cvall = at("cvall", 8 * SEQ, W0 + 36)[:, :].rearrange("p (n f) -> p n f", n=8)
    qdecT, ktail = eight("qdecT", 36), eight("ktail", 40)
    qk = eight("qk", 44)
    vb = eight("vb", 48)
    qkT, off1 = eight("qkT", 52), eight("off1", 52)
    A = eight("A", 56)
    dT, T = eight("dT", 60), eight("T", 60)
    dA, TT = eight("dA", 64), eight("TT", 64)
    gm, Pm = eight("gm", 68), eight("Pm", 68)
    vnew = at("vnew", GH * BH, W0 + 0)[:, :].rearrange("p (h d) -> p h d", h=GH)
    osq = at("osq", 512, W0 + 4)
    otmp = at("otmp", 512, W0 + 6)
    h2hi = at("h2hi", TB * D, W0 + 0, F32R)[:, :].rearrange("p (b d) -> p b d", b=TB)
    h2lo = at("h2lo", TB * D, W0 + 8, F32R)[:, :].rearrange("p (b d) -> p b d", b=TB)
    sel = at("sel", TB * P, W0 + 20, F32R)[:, :].rearrange("p (b s) -> p b s", b=TB)
    selT = at("selT", TB * P, W0 + 21, F32R)
    yhi = at("yhi", D, W0 + 22, F32R)
    ylo = at("ylo", D, W0 + 26, F32R)
    hTf = at("hTf", KT * SEQ, W0 + 34)[:, :].rearrange("p (k t) -> p k t", k=KT)
    gain3 = at("gain3", D, W0 + 42)
    H3 = at("H3", TB * D, W0 + 46)[:, :].rearrange("p (b d) -> p b d", b=TB)
    small_at = [0]

    def small(n):
        a = par[:, small_at[0]:small_at[0] + n]
        small_at[0] += n
        return a
    ms, rs = small(2), small(2)
    halfneg = small(8)
    sink8, mx, nm, es, ssum, rsum = (small(8) for _ in range(6))
    sink16 = small(HEADS)
    convw = small(P)
    convw_v = convw.rearrange("p (w t) -> p w t", w=4)
    alog, dtb = small(VH), small(VH)
    wr = small(KT * NE)
    g32, beta, gc, egc, ebeta, etail, sa, sb_ = (small(2 * VH) for _ in range(8))
    egl = small(4 * VH)
    r8, ss8 = small(8), small(8)
    lg, top, oh1, oh2, tmp8, cmb, pos, msk = (small(TB * NE) for _ in range(8))
    topi = small(TB * NE)
    gt, e2, cnt = small(4), small(4), small(1)
    assert small_at[0] <= 820
    wba = at("wba", KT * 2 * VH, W0 + 72.0 - 1)
    npass = at("npass", 1, 131.25, I32)
    ngain = at("ngain", BH, W0 + 72)
    cwrow = at("cwrow", P, 131.5)

    def tb_(name):
        return tabs[:, TABLE[name]:TABLE[name] + P]

    ident = tb_("ident")

    with ExitStack() as ctx:
        def sem(name):
            if name not in sems:
                sems[name] = ctx.enter_context(nc.semaphore(name))
            return sems[name]

        landed = [sem(f"panel_landed{n}") for n in range(RAW)]
        hi_ready, lo_ready, panel_used = sem("hi_ready"), sem("lo_ready"), sem("panel_used")
        loads = sem("params_loaded")
        x_loaded, gain_loaded, tab_loaded = sem("x_loaded"), sem("gain_loaded"), sem("tab_loaded")
        phase_b_params = sem("phase_b_params")

        panels = []

        def wide(w, n0):
            for half in range(2):
                panels.append((w[half * 512:half * 512 + 512, n0:n0 + 512].rearrange("(k p) n -> p k n", p=P), 4))

        def narrow(w, n0):
            panels.append((w[:, n0:n0 + 256].rearrange("(k p) n -> p k n", p=P), 8))

        def rows(w, k0):
            panels.append((w[k0:k0 + 256, :].rearrange("(k p) n -> p k n", p=P), 2))

        for c in range(3):
            wide(w_qkv, c * 512)
        P_WO = len(panels)
        for c in range(4):
            rows(w_o, c * 256)
        P_FFN = len(panels)
        FCH = DFF // 256
        for c in range(FCH + 1):
            if c < FCH:
                narrow(f_gate, c * 256)
                narrow(f_up, c * 256)
            if c:
                rows(f_down, (c - 1) * 256)
        P_IN = len(panels)
        for g in range(GROUPS):
            narrow(w_in, g * 256)
            narrow(w_in, QK_DIM + g * 256)
            wide(w_in, 2 * QK_DIM + g * 512)
            wide(w_in, 2 * QK_DIM + V_DIM + g * 512)
        P_DNO = len(panels)
        for c in range(V_DIM // 256):
            rows(dn_w_o, c * 256)
        P_MOE = len(panels)
        EP = 6 * ECH
        assert EP % RAW == 0 and EP % SPLIT == 0

        def slot(t, n, ring):
            return t[:, (n % ring) * PANEL:(n % ring + 1) * PANEL]

        class Split:
            def __init__(self, one):
                self.one, self.n = one, 0

            def upto(self, n):
                while self.n <= min(n, P_MOE - 1):
                    self.one(self.n, self.n)
                    self.n += 1

        def chunk_panel(sp, it, c, i, src):
            sp.wait_ge(lo_ready, it * EP + c * 6 + (P_MOE + 10 - 12 + i - RAW + 1))
            n = P_MOE + 10 + i
            sp.dma_start(slot(raw, n, RAW).rearrange("p (k n) -> p k n", k=src.shape[1] // P),
                         src.rearrange("a (k p) n -> p (a k) n", p=P)).then_inc(landed[n % RAW], 16)

        block = ctx.enter_context(nc.Block())

        @block.sync
        def _(sp):
            sp.dma_start(X, x[0].rearrange("(b p) d -> p b d", p=P)).then_inc(x_loaded, 16)
            sp.dma_start(gain[:, :], norm_g[0, 0:1, :].partition_broadcast(P)[:, 0]).then_inc(gain_loaded, 16)
            sp.dma_start(tabs[:, :], tab).then_inc(tab_loaded, 16)

            def panel(n, src, free):
                if free is not None:
                    sp.wait_ge(lo_ready, free)
                k = src.shape[1]
                sp.dma_start(slot(raw, n, RAW).rearrange("p (k n) -> p k n", k=k), src).then_inc(landed[n % RAW], 16)

            def upto(n0, n1):
                for n in range(n0, n1):
                    panel(n, panels[n][0], n - RAW + 1 if n >= RAW else None)

            upto(0, 2)
            sp.dma_start(bqkv[:, :], b_qkv.partition_broadcast(P)[:, 0]).then_inc(loads, 16)
            sp.dma_start(abias, ali.rearrange("n p f -> p n f")).then_inc(loads, 16)
            sp.dma_start(sink16, sinks.partition_broadcast(P)[:, 0]).then_inc(loads, 16)
            sp.dma_start(cwrow[:, :], conv_w[0].rearrange("w (t c) -> (w t) c", c=P)).then_inc(loads, 16)
            sp.dma_start(alog, a_log.partition_broadcast(P)[:, 0]).then_inc(loads, 16)
            sp.dma_start(dtb, dt_bias.partition_broadcast(P)[:, 0]).then_inc(loads, 16)
            sp.dma_start(wr.rearrange("p (k e) -> p k e", k=KT), w_router[0].rearrange("(k p) e -> p k e", p=P)).then_inc(loads, 16)
            upto(2, P_WO)
            sp.wait_ge(sem("h_ready"), 1)
            sp.dma_start(gain[:, :], norm_g[0, 1:2, :].partition_broadcast(P)[:, 0]).then_inc(gain_loaded, 16)
            upto(P_WO, P_FFN + 3)
            sp.wait_ge(sem("h_ready"), 2)
            sp.dma_start(gain[:, :], norm_g[1, 0:1, :].partition_broadcast(P)[:, 0]).then_inc(gain_loaded, 16)
            sp.dma_start(wba[:, :].rearrange("p (k n) -> p k n", k=KT),
                         w_in[:, IN_DIM - 2 * VH:].rearrange("(k p) n -> p k n", p=P)).then_inc(phase_b_params, 16)
            sp.dma_start(ngain[:, :], dn_norm_g.partition_broadcast(P)[:, 0]).then_inc(phase_b_params, 16)
            upto(P_FFN + 3, P_DNO)
            upto(P_DNO, P_DNO + 3)
            sp.wait_ge(sem("o_done"), TB * GROUPS)
            sp.dma_start(gain3[:, :], norm_g[1, 1:2, :].partition_broadcast(P)[:, 0]).then_inc(gain_loaded, 16)
            upto(P_DNO + 3, P_MOE)

            def expert_panel(e, it, local, src):
                sp.wait_ge(lo_ready, it * EP + (P_MOE + local - RAW + 1))
                n = P_MOE + local
                k = src.shape[1]
                sp.dma_start(slot(raw, n, RAW).rearrange("p (k n) -> p k n", k=k), src).then_inc(landed[n % RAW], 16)

            def up_panels(e, it, local, c):
                for w in (e_gate, e_up):
                    for half in range(2):
                        src = w[bass.ds(e, 1), half * 512:half * 512 + 512, bass.ds(c * 512, 512)]
                        expert_panel(e, it, local, src.rearrange("a (k p) n -> p (a k) n", p=P))
                        local = local + 1

            def down_panels(e, it, local, c):
                for half in range(2):
                    src = e_down[bass.ds(e, 1), bass.ds(c * 512 + half * 256, 256), :]
                    expert_panel(e, it, local + half, src.rearrange("a (k p) n -> p (a k) n", p=P))

            sp.wait_ge(sem("npass_ready"), 1)
            passes = sp.value_load(npass[0:1, 0:1], min_val=1, max_val=2)
            with sp.Fori(0, passes) as q:
                with sp.Fori(0, NE) as e:
                    it = q * NE + e
                    up_panels(e, it, 0, 0)
                    up_panels(e, it, 4, 1)
                    down_panels(e, it, 8, 0)
                    with sp.Fori(2, ECH) as c:
                        for i, w in enumerate((e_gate, e_gate, e_up, e_up)):
                            src = w[bass.ds(e, 1), i % 2 * 512:i % 2 * 512 + 512, bass.ds(c * 512, 512)]
                            chunk_panel(sp, it, c, i, src)
                        for i in range(2):
                            src = e_down[bass.ds(e, 1), bass.ds(c * 512 + (i * 256 - 512), 256), :]
                            chunk_panel(sp, it, c, 4 + i, src)
                    down_panels(e, it, EP - 2, ECH - 1)
            sp.wait_ge(sem("acc_added"), passes * (NE * 4) + 1)
            sp.dma_start(gain3[:, :], final_norm_g.rearrange("(a d) -> a d", a=1).partition_broadcast(P)[:, 0]).then_inc(gain_loaded, 16)
            sp.wait_ge(sem("h_ready"), 5)
            sp.dma_start(out[0].rearrange("(b p) d -> p b d", p=P), H3).then_inc(sem("out_stored"), 16)
            sp.wait_ge(sem("out_stored"), 16)

        @block.gpsimd
        def _(pool):
            pool.memset(halfneg, -0.5).then_inc(sem("pool_const"), 1)
            pool.wait_ge(sem("pool_const"), 1)

            def rsqrt(dst, src, n, count):
                pool.wait_ge(sem("ms_ready"), count)
                pool.tensor_tensor(dst, src, halfneg[:, 0:n], ALU.pow).then_inc(sem("rs_ready"), 1)

            k = 0
            for _n in range(3):
                k += 1
                rsqrt(rs, ms, 2, k)
            for g in range(GROUPS):
                k += 1
                rsqrt(r8, ss8, 8, k)
                pool.wait_ge(sem("qkn_ready"), g + 1)
                if g:
                    pool.wait_ge(sem("o_done"), TB * g)
                for src0, dst, fac in ((2, kbe, ebeta), (0, qdec, egc), (2, ktail, etail)):
                    for b in range(TB):
                        s_ = qk[:, 4 * b + src0:4 * b + src0 + 2, :].unsqueeze(2).broadcast_to([P, 2, 2, P])
                        f_ = fac[:, b * VH + g * GH:b * VH + g * GH + GH].rearrange("p (k r) -> p k r", r=2)
                        f_ = f_.unsqueeze(3).broadcast_to([P, 2, 2, P])
                        d_ = dst[:, 4 * b:4 * b + 4, :].rearrange("p (k r) f -> p k r f", r=2)
                        i = pool.tensor_tensor(d_, s_, f_, ALU.mult)
                    i.then_inc(sem("scaled"), 1)
                pool.wait_ge(sem("A_ready"), g + 1)
                for lv in range(1, 6):
                    o = off0 if lv % 2 else off1
                    if lv >= 3:
                        pool.wait_ge(sem("P_psum"), (g * 5 + lv - 2) * 2)
                    m_ = tb_(f"level{lv}").unsqueeze(1).broadcast_to([P, 8, P])
                    pool.tensor_tensor(o, A, m_, ALU.mult).then_inc(sem("off_ready"), 1)
                for b in range(TB):
                    k += 1
                    rsqrt(r8[:, 0:4], ss8[:, 0:4], 4, k)
            for _n in range(2):
                k += 1
                rsqrt(rs, ms, 2, k)

        @block.scalar
        def _(act):
            chain = [0]

            def link(i):
                chain[0] += 1
                i.then_inc(sem("act_chain"), 1)
                act.wait_ge(sem("act_chain"), chain[0])

            def hi(n, v):
                act.wait_ge(landed[n % RAW], 16 * (v // RAW + 1))
                if v >= SPLIT:
                    act.wait_ge(panel_used, v - SPLIT + 1)
                act.copy(slot(whi, n, SPLIT), slot(raw, n, RAW)).then_inc(hi_ready, 1)

            hi_panels = Split(hi)

            def split_hi(norm, first):
                for j in range(4):
                    act.wait_ge(sem("hT_psum"), 4 * norm + j + 1)
                    act.copy(xhi[:, j * 512:(j + 1) * 512], bank[j]).then_inc(sem("xhi_ready"), 1)

            hi_panels.upto(2)
            split_hi(0, True)
            hi_panels.upto(P_WO - 1 - 0)
            act.wait_ge(sem("qkv_ready"), 3)
            act.copy(vsh[HD:P, 0, :], qkv[0:HD, 0, QKV - 256:])
            act.copy(vsh[0:HD, 1, :], qkv[HD:P, 0, QKV - 256:])
            act.copy(vsh[HD:P, 1, :], qkv[0:HD, 1, QKV - 256:]).then_inc(sem("vsh_ready"), 1)
            for f in range(10):
                act.wait_ge(sem("head_psum"), f + 1)
                if f < 2:
                    src = bank[f % 4][0:HD, :].rearrange("p (h t) -> p h t", h=2)
                    dst = kT[:, 2 * f:2 * f + 2, CHUNK:]
                else:
                    src = bank[f % 4][0:HD, :].rearrange("p (h n q) -> p h n q", h=2, n=NCH)
                    dst = qT[:, :, 2 * f - 4:2 * f - 2, :].rearrange("p n h q -> p h n q")
                act.copy(dst, src).then_inc(sem("head_sb"), 1)
            hi_panels.upto(P_WO + 2)
            for n in range(NCH):
                act.wait_ge(sem("max_ready"), n + 1)
                act.activation(es, es, ACT.Exp)
                for j in range(PAIRS):
                    s_ = sc[:, n % 2, j * P:(j + 1) * P]
                    i = act.activation(s_, s_, ACT.Exp, bias=nm[:, j:j + 1], scale=1.0, accum_out=ssum[:, j:j + 1])
                i.then_inc(sem("exp_ready"), 1)
                act.wait_ge(sem("pT_psum"), n + 1)
                for h in range(2):
                    i = act.copy(pT[:, 4 * h:4 * h + 4, :], bank[h].rearrange("p (j c) -> p j c", j=4))
                i.then_inc(sem("pT_ready"), 1)
                act.wait_ge(sem("oT_psum"), n + 1)
                o_ = bank[2 + n % 2].rearrange("p (j t) -> p j t", j=PAIRS)
                act.copy(xhi[:, :].rearrange("p (j t) -> p j t", j=PAIRS)[:, :, n * CHUNK:(n + 1) * CHUNK], o_)\
                    .then_inc(sem("oThi_ready"), 1)
            hi_panels.upto(P_FFN + 2)
            split_hi(1, False)
            for c in range(FCH + 1):
                if c < FCH:
                    up = P_FFN + (3 * c if c else 1)
                    hi_panels.upto(up + 2)
                    act.wait_ge(panel_used, up + 1)
                    for b in range(TB):
                        i = act.activation(sil[:, b * 256:b * 256 + 256], bank[b][:, 0:256], ACT.Silu)
                    i.then_inc(sem("sil_ready"), 1)
                    hi_panels.upto(up + (3 if c else 2))
                    act.wait_ge(sem("hidT_psum"), c + 1)
                    act.copy(hhi[:, :], bank[2]).then_inc(sem("hhi_ready"), 1)
            hi_panels.upto(P_IN + 2)
            split_hi(2, False)
            act.wait_ge(phase_b_params, 32)
            act.copy(hhi[:, 0:256], wba[:, :]).then_inc(sem("wba_hi"), 1)
            act.wait_ge(loads, 112)
            act.activation(alog, alog, ACT.Exp)
            act.wait_ge(sem("ba_psum"), 1)
            act.activation(beta.rearrange("p (b h) -> p b h", b=TB),
                           bank[4][:, 0:64].rearrange("p (b n) -> p b n", b=TB)[:, :, 0:VH], ACT.Exp, scale=-1.0)\
                .then_inc(sem("gate_act"), 1)
            act.wait_ge(sem("gate_dve"), 1)
            link(act.activation(sb_, sb_, ACT.Exp, scale=-1.0))
            act.activation(sb_, sb_, ACT.Ln, bias=1.0).then_inc(sem("gate_act"), 1)
            act.wait_ge(sem("gsum_psum"), 1)
            act.activation(egl, bank[5][:, 64:128], ACT.Exp)
            act.activation(egc, bank[5][:, 0:32], ACT.Exp)
            act.copy(gc, bank[5][:, 0:32]).then_inc(sem("gate_act"), 1)
            act.wait_ge(sem("gate_dve"), 3)
            act.activation(etail, etail, ACT.Exp).then_inc(sem("gate_act"), 1)
            for g in range(GROUPS):
                base_p = P_IN + 6 * g
                hi_panels.upto(base_p + 3)
                act.wait_ge(panel_used, base_p + 2)
                if g:
                    act.wait_ge(sem("o_done"), TB * g)
                for b in range(TB):
                    i = act.copy(prj[:, 0, b, :], bank[b])
                i.then_inc(sem("prj_ready"), 1)
                hi_panels.upto(base_p + 5)
                act.wait_ge(panel_used, base_p + 4)
                for b in range(TB):
                    i = act.copy(prj[:, 1, b, :], bank[2 + b])
                i.then_inc(sem("prj_ready"), 1)
                hi_panels.upto(base_p + 7)
                act.wait_ge(panel_used, base_p + 6)
                for b in range(TB):
                    i = act.activation(oall[:, b, g * 512:(g + 1) * 512], bank[4 + b], ACT.Silu)
                i.then_inc(sem("z_ready"), 1)
                hi_panels.upto(base_p + 8)
                act.wait_ge(sem("conv_ready"), g + 1)
                act.activation(cvall, cvall, ACT.Silu).then_inc(sem("convs_ready"), 1)
                act.wait_ge(sem("back_psum"), 2 * g + 1)
                for b in range(TB):
                    i = act.copy(qk[:, 4 * b:4 * b + 4, :], bank[2 + b].rearrange("p (n f) -> p n f", n=4))
                i.then_inc(sem("qk_ready"), 1)
                act.wait_ge(sem("qkT_psum"), g + 1)
                for b in range(TB):
                    i = act.copy(qkT[:, 4 * b:4 * b + 4, :], bank[6 + b].rearrange("p (n f) -> p n f", n=4))
                i.then_inc(sem("qkT_ready"), 1)
                act.wait_ge(sem("dec_ready"), g + 1)
                act.activation(dA, dA, ACT.Exp, scale=-1.0)
                act.activation(dT, dT, ACT.Exp).then_inc(sem("decay_ready"), 1)
                act.wait_ge(sem("qdT_psum"), g + 1)
                for b in range(TB):
                    i = act.copy(qdecT[:, 4 * b:4 * b + 4, :], bank[4 + b].rearrange("p (n f) -> p n f", n=4))
                i.then_inc(sem("qdT_ready"), 1)
                for b in range(TB):
                    act.wait_ge(sem("TT0_psum"), 2 * g + b + 1)
                    act.copy(TT[:, 4 * b:4 * b + 4, :], bank[b].rearrange("p (n f) -> p n f", n=4))\
                        .then_inc(sem("TT0_ready"), 1)
                for lv in range(1, 6):
                    u = g * 5 + lv - 1
                    for b in range(TB):
                        act.wait_ge(sem("P_psum"), 2 * u + b + 1)
                        act.copy(Pm[:, 4 * b:4 * b + 4, :], bank[2 + b].rearrange("p (n f) -> p n f", n=4))\
                            .then_inc(sem("P_ready"), 1)
                    if lv < 5:
                        v_ = g * 4 + lv - 1
                        for b in range(TB):
                            act.wait_ge(sem("T_psum"), 2 * v_ + b + 1)
                            act.copy(T[:, 4 * b:4 * b + 4, :], bank[b].rearrange("p (n f) -> p n f", n=4))\
                                .then_inc(sem("T_ready"), 1)
                act.wait_ge(sem("wT_psum"), g + 1)
                for b in range(TB):
                    i = act.copy(wT[:, 4 * b:4 * b + 4, :], bank[4 + b].rearrange("p (n f) -> p n f", n=4))
                i.then_inc(sem("wT_ready"), 1)
                for n in range(NCH):
                    r0 = n % 2 * CHUNK
                    act.wait_ge(sem("v_psum"), g * NCH + n + 1)
                    act.copy(vnew[r0:r0 + CHUNK, :, :], bank[0][r0:r0 + CHUNK, :].rearrange("p (h d) -> p h d", h=GH))\
                        .then_inc(sem("v_ready"), 1)
            hi_panels.upto(P_DNO + 2)
            for f in range(8):
                act.wait_ge(sem("on_psum"), f + 1)
                if f >= 4:
                    act.wait_ge(panel_used, P_DNO + f - 4 + 1)
                act.copy(xhi[:, (f % 4) * 512:(f % 4 + 1) * 512], bank[f % 4]).then_inc(sem("onhi_ready"), 1)
                hi_panels.upto(P_DNO + f + 2)
            hi_panels.upto(P_MOE - 1)
            act.wait_ge(sem("h_ready"), 4)
            act.copy(h2hi, H3).then_inc(sem("h2hi_ready"), 1)
            for j in range(4):
                act.wait_ge(sem("hT_psum"), 13 + j)
                act.copy(hTf[:, 2 * j:2 * j + 2, :], bank[j].rearrange("p (k t) -> p k t", k=2)).then_inc(sem("hTf_ready"), 1)
            act.wait_ge(sem("route_dve"), 1)
            act.activation(e2[:, 0:2], e2[:, 0:2], ACT.Exp).then_inc(sem("route_act"), 1)
            act.wait_ge(sem("npass_ready"), 1)
            passes = act.value_load(npass[0:1, 0:1], min_val=1, max_val=2)

            def ehi(it, local, more=0):
                n = P_MOE + local
                act.wait_ge(landed[n % RAW], it * (16 * EP // RAW) + more * 16 + 16 * (n // RAW + 1))
                act.wait_ge(panel_used, it * EP + more * 6 + (n - SPLIT + 1))
                act.copy(slot(whi, n, SPLIT), slot(raw, n, RAW)).then_inc(hi_ready, 1)

            def silu(it, local, more=0):
                act.wait_ge(panel_used, it * EP + more * 6 + (P_MOE + local + 1))
                act.activation(sil[:, :], bank[0], ACT.Silu).then_inc(sem("esil_ready"), 1)

            def hidden_hi(u):
                act.wait_ge(sem("ehT_psum"), u + 1)
                act.copy(hhi[:, :], bank[2]).then_inc(sem("ehhi_ready"), 1)

            with act.Fori(0, passes) as q:
                with act.Fori(0, NE) as e:
                    it = q * NE + e
                    for i in range(3):
                        ehi(it, i)
                    act.wait_ge(sem("selT_psum"), it + 1)
                    act.copy(selT[:, :], bank[5][:, 0:256]).then_inc(sem("selT_ready"), 1)
                    for h in range(2):
                        act.wait_ge(sem("gath_psum"), it * 2 + (h + 1))
                        act.copy(xhi[:, h * 512:(h + 1) * 512], bank[6 + h]).then_inc(sem("gxhi_ready"), 1)
                    ehi(it, 3)
                    ehi(it, 4)
                    ehi(it, 5)
                    silu(it, 3)
                    hidden_hi(it * ECH)
                    for i in range(6, 10):
                        ehi(it, i)
                    silu(it, 7)
                    ehi(it, 10)
                    ehi(it, 11)
                    hidden_hi(it * ECH + 1)
                    with act.Fori(2, ECH - 1) as c:
                        for i in range(12, 16):
                            ehi(it, i, c - 2)
                        silu(it, 13, c - 2)
                        ehi(it, 16, c - 2)
                        ehi(it, 17, c - 2)
                        hidden_hi(it * ECH + c)
                    for i in range(36, 40):
                        ehi(it, i)
                    silu(it, 37)
                    ehi(it, 40)
                    ehi(it, 41)
                    hidden_hi(it * ECH + (ECH - 1))
                    act.wait_ge(panel_used, it * EP + (P_MOE + EP))
                    for h in range(2):
                        i = act.copy(yhi[:, h * 512:(h + 1) * 512], bank[3 + h])
                    i.then_inc(sem("yhi_ready"), 1)

        @block.vector
        def _(dve):
            chain = [0]

            def link(i):
                chain[0] += 1
                i.then_inc(sem("dve_chain"), 1)
                dve.wait_ge(sem("dve_chain"), chain[0])

            def lo(n, v):
                dve.wait_ge(hi_ready, v + 1)
                dve.tensor_tensor(slot(wlo, n, SPLIT), slot(raw, n, RAW), slot(whi, n, SPLIT).bitcast(F32),
                                  ALU.subtract).then_inc(lo_ready, 1)

            lo_panels = Split(lo)
            rsn = [0]

            def rsqrt(dst):
                rsn[0] += 1
                dst.then_inc(sem("ms_ready"), 1)
                dve.wait_ge(sem("rs_ready"), rsn[0])

            def norm(n, g_, h_):
                dve.wait_ge(gain_loaded, 16 * (n + 1))
                for b in range(TB):
                    i = dve.tensor_tensor_reduce(h_[:, b, :], X[:, b, :], X[:, b, :], 1.0, 0.0, ALU.mult, ALU.add,
                                                 ms[:, b:b + 1])
                link(i)
                rsqrt(dve.tensor_scalar(ms, ms, 1.0 / D, EPS, ALU.mult, ALU.add))
                for b in range(TB):
                    i = dve.scalar_tensor_tensor(out=h_[:, b, :], in0=X[:, b, :], scalar=rs[:, b:b + 1], in1=g_,
                                                 op0=ALU.mult, op1=ALU.mult)
                i.then_inc(sem("h_ready"), 1)

            def split_lo(norm):
                for j in range(4):
                    dve.wait_ge(sem("xhi_ready"), 4 * norm + j + 1)
                    s_ = slice(j * 512, (j + 1) * 512)
                    dve.tensor_tensor(xlo[:, s_], bank[j], xhi[:, s_].bitcast(F32), ALU.subtract)\
                        .then_inc(sem("xlo_ready"), 1)

            def add_y(used):
                dve.wait_ge(panel_used, used)
                for b in range(TB):
                    for h in range(2):
                        s_ = X[:, b, h * 512:(h + 1) * 512]
                        i = dve.tensor_tensor(s_, s_, bank[4 + 2 * b + h], ALU.add)
                link(i)

            dve.memset(kT[:, :, 0:CHUNK], 0.0)
            dve.memset(vsh[0:HD, 0, :], 0.0).then_inc(sem("pads_ready"), 1)
            dve.wait_ge(x_loaded, 16)
            norm(0, gain[:, :], H)
            lo_panels.upto(2)
            split_lo(0)
            dve.wait_ge(loads, 112)
            sk2 = sink16.rearrange("p (j r) -> p r j", r=2)
            for r in range(2):
                i = dve.tensor_copy(sink8[r * HD:(r + 1) * HD, :], sk2[r * HD:(r + 1) * HD, r, :])
            link(i)
            for c in range(3):
                lo_panels.upto(min(2 * c + 3, P_WO - 1))
                dve.wait_ge(panel_used, 2 * c + 2)
                for b in range(TB):
                    i = dve.tensor_tensor(qkv[:, b, c * 512:(c + 1) * 512], bank[4 + 2 * (c % 2) + b],
                                          bqkv[:, c * 512:(c + 1) * 512], ALU.add)
                i.then_inc(sem("qkv_ready"), 1)
            lo_panels.upto(P_WO + 2)
            for n in range(NCH):
                dve.wait_ge(sem("score_psum"), n + 1)
                if n >= 2:
                    dve.wait_ge(sem("pT_psum"), n - 1)
                for h in range(2):
                    i = dve.scalar_tensor_tensor(out=sc[:, n % 2, h * 512:(h + 1) * 512], in0=bank[4 + 2 * (n % 2) + h],
                                                 scalar=HD ** -0.5, in1=abias[:, 1 if n else 0, h * 512:(h + 1) * 512],
                                                 op0=ALU.mult, op1=ALU.add)
                link(i)
                s3 = sc[:, n % 2, :].rearrange("p (j k) -> p j k", j=PAIRS)
                link(dve.tensor_reduce(mx, s3, AX_X, ALU.max))
                link(dve.tensor_tensor(mx, mx, sink8, ALU.max))
                dve.tensor_scalar(nm, mx, -1.0, None, ALU.mult)
                dve.tensor_tensor(es, sink8, mx, ALU.subtract).then_inc(sem("max_ready"), 1)
                dve.wait_ge(sem("exp_ready"), n + 1)
                link(dve.tensor_tensor(ssum, ssum, es, ALU.add))
                link(dve.reciprocal(rsum, ssum))
                dve.tensor_tensor(s3, s3, rsum.unsqueeze(2).broadcast_to([P, PAIRS, P]), ALU.mult)\
                    .then_inc(sem("probs_ready"), 1)
                dve.wait_ge(sem("oThi_ready"), n + 1)
                x3 = xlo[:, :].rearrange("p (j t) -> p j t", j=PAIRS)[:, :, n * CHUNK:(n + 1) * CHUNK]
                h3 = xhi[:, :].bitcast(F32).rearrange("p (j t) -> p j t", j=PAIRS)[:, :, n * CHUNK:(n + 1) * CHUNK]
                dve.tensor_tensor(x3, bank[2 + n % 2].rearrange("p (j t) -> p j t", j=PAIRS), h3, ALU.subtract)\
                    .then_inc(sem("oTlo_ready"), 1)
            lo_panels.upto(P_FFN + 2)
            add_y(P_FFN)
            norm(1, gain[:, :], H)
            split_lo(1)
            for c in range(FCH + 1):
                if c < FCH:
                    up = P_FFN + (3 * c if c else 1)
                    lo_panels.upto(up + 2)
                    dve.wait_ge(sem("sil_ready"), c + 1)
                    for b in range(TB):
                        s_ = slice(b * 256, b * 256 + 256)
                        i = dve.tensor_tensor(hid[:, s_], bank[b][:, 256:512], sil[:, s_], ALU.mult)
                    i.then_inc(sem("hid_ready"), 1)
                    lo_panels.upto(up + (3 if c else 2))
                    dve.wait_ge(sem("hhi_ready"), c + 1)
                    dve.tensor_tensor(hlo[:, :], bank[2], hhi[:, :].bitcast(F32), ALU.subtract)\
                        .then_inc(sem("hlo_ready"), 1)
            lo_panels.upto(P_IN + 2)
            add_y(P_IN)
            norm(2, gain[:, :], H)
            split_lo(2)
            dve.wait_ge(sem("wba_hi"), 1)
            dve.tensor_tensor(hlo[:, 0:256], wba[:, :], hhi[:, 0:256].bitcast(F32), ALU.subtract).then_inc(sem("wba_lo"), 1)
            dve.wait_ge(sem("cw_psum"), 1)
            dve.tensor_copy(convw, bank[6][:, 0:P])
            dve.wait_ge(sem("gate_act"), 1)
            a2 = bank[4][:, 0:64].rearrange("p (b n) -> p b n", b=TB)[:, :, VH:]
            two = lambda t: t.rearrange("p (b h) -> p b h", b=TB)
            twice = lambda t: t.unsqueeze(1).broadcast_to([P, TB, VH])
            dve.tensor_scalar(beta, beta, 1.0, None, ALU.add)
            link(dve.tensor_tensor(two(sa), a2, twice(dtb), ALU.add))
            dve.reciprocal(beta, beta)
            link(dve.tensor_scalar(sb_, sa, -1.0, None, ALU.mult))
            dve.tensor_tensor(sb_, sa, sb_, ALU.max).then_inc(sem("gate_dve"), 1)
            dve.wait_ge(sem("gate_act"), 2)
            link(dve.scalar_tensor_tensor(out=sb_, in0=sa, scalar=0.0, in1=sb_, op0=ALU.max, op1=ALU.add))
            dve.scalar_tensor_tensor(out=two(g32), in0=two(sb_), scalar=-1.0, in1=twice(alog),
                                     op0=ALU.mult, op1=ALU.mult).then_inc(sem("gate_dve"), 1)
            dve.wait_ge(sem("gate_act"), 3)
            dve.scalar_tensor_tensor(out=ebeta, in0=beta, scalar=-1.0, in1=egc, op0=ALU.mult, op1=ALU.mult)
            dve.tensor_tensor(etail, bank[5][:, 32:64], gc, ALU.subtract).then_inc(sem("gate_dve"), 1)
            dve.wait_ge(sem("gate_act"), 4)
            for g in range(GROUPS):
                base_p = P_IN + 6 * g
                lo_panels.upto(base_p + 5)
                lo_panels.upto(base_p + 8)
                dve.wait_ge(sem("ch_psum"), g + 1)
                for w in range(3, -1, -1):
                    s_ = 3 - w
                    for t in range(8):
                        tile = (2 * g + t) if t < 2 else (8 + 2 * g + t - 2) if t < 4 else (16 + 4 * g + t - 4)
                        src = bank[(6, 7, 0, 1)[t // 2]][:, t % 2 * SEQ:(t % 2 + 1) * SEQ - s_]
                        k_ = convw_v[:, w, tile:tile + 1]
                        if s_ == 0:
                            i = dve.tensor_scalar(cvall[:, t, :], src, k_, None, ALU.mult)
                        else:
                            i = dve.scalar_tensor_tensor(out=cvall[:, t, s_:], in0=src, scalar=k_, in1=cvall[:, t, s_:],
                                                         op0=ALU.mult, op1=ALU.add)
                    if w:
                        link(i)
                i.then_inc(sem("conv_ready"), 1)
                dve.wait_ge(sem("back_psum"), 2 * g + 2)
                for b in range(TB):
                    be = beta[:, b * VH + g * GH:b * VH + g * GH + GH].unsqueeze(2).broadcast_to([P, GH, P])
                    i = dve.tensor_tensor(vb[:, 4 * b:4 * b + 4, :], bank[4 + b].rearrange("p (n f) -> p n f", n=4), be, ALU.mult)
                i.then_inc(sem("vb_ready"), 1)
                dve.wait_ge(sem("qk_ready"), g + 1)
                link(dve.tensor_tensor(A, qk, qk, ALU.mult))
                link(dve.tensor_reduce(ss8, A, AX_X, ALU.add))
                rsqrt(dve.tensor_scalar(ss8, ss8, EPS, None, ALU.add))
                r3 = r8.rearrange("p (b n) -> p b n", b=TB)
                link(dve.tensor_scalar(r3[:, :, 0:2], r3[:, :, 0:2], BH ** -0.5, None, ALU.mult))
                link(dve.tensor_tensor(qk, qk, r8.unsqueeze(2).broadcast_to([P, 8, P]), ALU.mult))
                for n in range(8):
                    b, h = divmod(n, GH)
                    i = dve.tensor_scalar(gm[:, n, :], tb_("cum"), g32[:, b * VH + g * GH + h:b * VH + g * GH + h + 1], None, ALU.mult)
                i.then_inc(sem("qkn_ready"), 1)
                dve.wait_ge(sem("R_psum"), g + 1)
                for n in range(8):
                    b, h = divmod(n, GH)
                    col = gc[:, b * VH + g * GH + h:b * VH + g * GH + h + 1]
                    r_ = bank[b][:, h * P:(h + 1) * P]
                    dve.scalar_tensor_tensor(out=dA[:, n, :], in0=r_, scalar=col, in1=tb_("off_strict"),
                                             op0=ALU.subtract, op1=ALU.add)
                    i = dve.scalar_tensor_tensor(out=dT[:, n, :], in0=r_, scalar=col, in1=tb_("off_upper"),
                                                 op0=ALU.subtract, op1=ALU.subtract)
                i.then_inc(sem("dec_ready"), 1)
                dve.wait_ge(sem("decay_ready"), g + 1)
                dve.wait_ge(sem("kk_psum"), g + 1)
                for n in range(8):
                    b, h = divmod(n, GH)
                    kk = bank[2 + b].rearrange("p (k m f) -> p k m f", k=2, m=2)[:, h // 2]
                    dve.scalar_tensor_tensor(out=A[:, n, :], in0=kk[:, 1, :], scalar=beta[:, b * VH + g * GH + h:b * VH + g * GH + h + 1],
                                             in1=dA[:, n, :], op0=ALU.mult, op1=ALU.mult)
                    i = dve.tensor_tensor(attnT[:, n, :], kk[:, 0, :], dT[:, n, :], ALU.mult)
                i.then_inc(sem("A_ready"), 1)
                dve.wait_ge(sem("A_ready"), g + 1)
                link(dve.tensor_tensor(T, A, tb_("level0").unsqueeze(1).broadcast_to([P, 8, P]), ALU.mult))
                dve.tensor_tensor(T, ident.unsqueeze(1).broadcast_to([P, 8, P]), T, ALU.subtract).then_inc(sem("T0_ready"), 1)
                for lv in range(1, 6):
                    u = g * 5 + lv - 1
                    for b in range(TB):
                        dve.wait_ge(sem("dTT_psum"), 2 * u + b + 1)
                        t_ = TT[:, 4 * b:4 * b + 4, :]
                        dve.tensor_tensor(t_, t_, bank[4 + b].rearrange("p (n f) -> p n f", n=4), ALU.subtract)\
                            .then_inc(sem("TT_ready"), 1)
                for n in range(NCH):
                    b = n // 2
                    if n < NCH - 1:
                        dve.wait_ge(sem("s_psum"), g * (NCH - 1) + n + 1)
                        for h in range(GH):
                            ps = bank[1][:, h * P:(h + 1) * P]
                            if n == 0:
                                i = dve.tensor_copy(S[:, h, :], ps)
                            else:
                                col = (n % 2) * 2 * VH + (n // 2) * VH + g * GH + h
                                i = dve.scalar_tensor_tensor(out=S[:, h, :], in0=S[:, h, :], scalar=egl[:, col:col + 1],
                                                             in1=ps, op0=ALU.mult, op1=ALU.add)
                        i.then_inc(sem("S_ready"), 1)
                    if n % 2:
                        dve.wait_ge(sem("o_psum"), g * TB + b + 1)
                        ob = bank[6 + b]
                        o3 = otmp[:, :].rearrange("p (h d) -> p h d", h=GH)
                        link(dve.tensor_copy(otmp[:, :], ob))
                        link(dve.tensor_tensor(osq[:, :], otmp[:, :], otmp[:, :], ALU.mult))
                        link(dve.tensor_reduce(ss8[:, 0:4], osq[:, :].rearrange("p (h d) -> p h d", h=GH), AX_X, ALU.add))
                        rsqrt(dve.tensor_scalar(ss8[:, 0:4], ss8[:, 0:4], 1.0 / BH, EPS, ALU.mult, ALU.add))
                        link(dve.tensor_tensor(o3, o3, r8[:, 0:4].unsqueeze(2).broadcast_to([P, GH, BH]), ALU.mult))
                        link(dve.tensor_tensor(o3, o3, ngain[:, :].unsqueeze(1).broadcast_to([P, GH, BH]), ALU.mult))
                        z_ = oall[:, b, g * 512:(g + 1) * 512]
                        dve.wait_ge(sem("z_ready"), g + 1)
                        dve.tensor_tensor(z_, z_, otmp[:, :], ALU.mult).then_inc(sem("o_done"), 1)
            lo_panels.upto(P_DNO + 2)
            for f in range(8):
                dve.wait_ge(sem("onhi_ready"), f + 1)
                s_ = slice((f % 4) * 512, (f % 4 + 1) * 512)
                dve.tensor_tensor(xlo[:, s_], bank[f % 4], xhi[:, s_].bitcast(F32), ALU.subtract).then_inc(sem("onlo_ready"), 1)
                lo_panels.upto(P_DNO + f + 2)
            lo_panels.upto(P_MOE - 1)
            add_y(P_MOE)
            norm(3, gain3[:, :], H3)
            dve.wait_ge(sem("h2hi_ready"), 1)
            dve.tensor_tensor(h2lo, H3, h2hi.bitcast(F32), ALU.subtract).then_inc(sem("h2lo_ready"), 1)
            dve.wait_ge(sem("logit_psum"), 1)
            link(dve.tensor_copy(lg, bank[4][:, 0:TB * NE]))
            topu = topi.bitcast(U32)
            for b in range(TB):
                i = dve.max(top[:, b * NE:(b + 1) * NE], lg[:, b * NE:(b + 1) * NE])
            link(i)
            for b in range(TB):
                i = dve.max_index(topu[:, b * NE:(b + 1) * NE], top[:, b * NE:(b + 1) * NE], lg[:, b * NE:(b + 1) * NE])
            link(i)
            link(dve.tensor_copy(tmp8, topu))
            t3 = top.rearrange("p (b e) -> p b e", b=TB)
            i3 = tmp8.rearrange("p (b e) -> p b e", b=TB)
            dve.tensor_tensor(e2[:, 0:2], t3[:, :, 1], t3[:, :, 0], ALU.subtract).then_inc(sem("route_dve"), 1)
            for b in range(TB):
                dve.tensor_scalar(oh1[:, b * NE:(b + 1) * NE], tb_("iota")[:, 0:NE], i3[:, b, 0:1], None, ALU.is_equal)
                i = dve.tensor_scalar(oh2[:, b * NE:(b + 1) * NE], tb_("iota")[:, 0:NE], i3[:, b, 1:2], None, ALU.is_equal)
            link(i)
            dve.tensor_tensor(msk, oh1, oh2, ALU.add).then_inc(sem("route_dve"), 1)
            dve.wait_ge(sem("route_act"), 1)
            link(dve.tensor_scalar(gt[:, 0:2], e2[:, 0:2], 1.0, None, ALU.add))
            link(dve.reciprocal(gt[:, 0:2], gt[:, 0:2]))
            link(dve.tensor_tensor(gt[:, 2:4], gt[:, 0:2], e2[:, 0:2], ALU.mult))
            for b in range(TB):
                s_ = slice(b * NE, (b + 1) * NE)
                i = dve.tensor_scalar(cmb[:, s_], oh1[:, s_], gt[:, b:b + 1], None, ALU.mult)
            link(i)
            for b in range(TB):
                s_ = slice(b * NE, (b + 1) * NE)
                i = dve.scalar_tensor_tensor(out=cmb[:, s_], in0=oh2[:, s_], scalar=gt[:, 2 + b:3 + b], in1=cmb[:, s_],
                                             op0=ALU.mult, op1=ALU.add)
            link(i)
            dve.wait_ge(sem("rank_psum"), 1)
            link(dve.tensor_tensor(pos, bank[5][:, 0:TB * NE], msk, ALU.mult))
            link(dve.tensor_scalar(pos, pos, -1.0, None, ALU.add))
            link(dve.tensor_reduce(cnt, bank[5][:, 16:16 + NE], AX_X, ALU.max))
            link(dve.tensor_scalar(cnt, cnt, float(P) + 0.5, 1.0, ALU.is_gt, ALU.add))
            link(dve.tensor_copy(npass[:, :], cnt))
            dve.tensor_copy(gt[:, 0:1], gt[:, 0:1]).then_inc(sem("npass_ready"), 1)
            dve.tensor_copy(gt[:, 1:2], gt[:, 1:2]).then_inc(sem("acc_added"), 1)
            dve.wait_ge(sem("npass_ready"), 1)
            passes = dve.value_load(npass[0:1, 0:1], min_val=1, max_val=2)

            def elo(it, local, more=0):
                n = P_MOE + local
                dve.wait_ge(hi_ready, it * EP + more * 6 + (n + 1))
                dve.tensor_tensor(slot(wlo, n, SPLIT), slot(raw, n, RAW), slot(whi, n, SPLIT).bitcast(F32),
                                  ALU.subtract).then_inc(lo_ready, 1)

            def hidden(u):
                dve.wait_ge(sem("esil_ready"), u + 1)
                dve.tensor_tensor(hid[:, :], bank[1], sil[:, :], ALU.mult).then_inc(sem("ehid_ready"), 1)

            def hidden_lo(u):
                dve.wait_ge(sem("ehhi_ready"), u + 1)
                dve.tensor_tensor(hlo[:, :], bank[2], hhi[:, :].bitcast(F32), ALU.subtract).then_inc(sem("ehlo_ready"), 1)

            with dve.Fori(0, passes) as q:
                with dve.Fori(0, NE) as e:
                    it = q * NE + e
                    for b in range(TB):
                        i = dve.tensor_scalar(sel[:, b, :], tb_("iota"), pos[:, bass.ds(e + b * NE, 1)], None, ALU.is_equal)
                    i.then_inc(sem("sel_ready"), 1)
                    for i in range(3):
                        elo(it, i)
                    for h in range(2):
                        dve.wait_ge(sem("gxhi_ready"), it * 2 + (h + 1))
                        s_ = slice(h * 512, (h + 1) * 512)
                        dve.tensor_tensor(xlo[:, s_], bank[6 + h], xhi[:, s_].bitcast(F32), ALU.subtract)\
                            .then_inc(sem("gxlo_ready"), 1)
                    elo(it, 3)
                    elo(it, 4)
                    elo(it, 5)
                    hidden(it * ECH)
                    hidden_lo(it * ECH)
                    for i in range(6, 10):
                        elo(it, i)
                    hidden(it * ECH + 1)
                    elo(it, 10)
                    elo(it, 11)
                    hidden_lo(it * ECH + 1)
                    with dve.Fori(2, ECH - 1) as c:
                        for i in range(12, 16):
                            elo(it, i, c - 2)
                        hidden(it * ECH + c)
                        elo(it, 16, c - 2)
                        elo(it, 17, c - 2)
                        hidden_lo(it * ECH + c)
                    for i in range(36, 40):
                        elo(it, i)
                    hidden(it * ECH + (ECH - 1))
                    elo(it, 40)
                    elo(it, 41)
                    hidden_lo(it * ECH + (ECH - 1))
                    dve.wait_ge(sem("yhi_ready"), it + 1)
                    for h in range(2):
                        s_ = slice(h * 512, (h + 1) * 512)
                        i = dve.tensor_tensor(ylo[:, s_], bank[3 + h], yhi[:, s_].bitcast(F32), ALU.subtract)
                    i.then_inc(sem("ylo_ready"), 1)
                    for k in range(4):
                        b, h = divmod(k, 2)
                        dve.wait_ge(sem("comb_psum"), it * 4 + (k + 1))
                        dve.wait_ge(sem("acc_added"), it * 4 + 1)
                        s_ = X[:, b, h * 512:(h + 1) * 512]
                        dve.scalar_tensor_tensor(out=s_, in0=bank[5 + k % 2], scalar=cmb[:, bass.ds(e + b * NE, 1)], in1=s_,
                                                 op0=ALU.mult, op1=ALU.add).then_inc(sem("acc_added"), 1)
                dve.tensor_scalar(pos, pos, -float(P), None, ALU.add).then_inc(sem("pos_moved"), 1)
                dve.wait_ge(sem("pos_moved"), q + 1)
            dve.wait_ge(sem("acc_added"), passes * (NE * 4) + 1)
            norm(4, gain3[:, :], H3)

        @block.tensor
        def _(pe):
            def triple(ps, lhs_hi, lhs_lo, n, cols, start, stop):
                wh, wl = slot(whi, n, SPLIT)[:, cols], slot(wlo, n, SPLIT)[:, cols]
                pe.matmul(ps, lhs_hi, wh, start=start, stop=False)
                pe.matmul(ps, lhs_hi, wl, start=False, stop=False)
                return pe.matmul(ps, lhs_lo, wh, start=False, stop=stop)

            def xT(k, b):
                s_ = slice(k * SEQ + b * P, k * SEQ + (b + 1) * P)
                return xhi[:, s_], xlo[:, s_]

            def use(n):
                pe.wait_ge(lo_ready, n + 1)

            def wide_panels(n, outs):
                for half in range(2):
                    use(n + half)
                    for b in range(TB):
                        for k in range(4):
                            kt = half * 4 + k
                            i = triple(outs[b], *xT(kt, b), n + half, slice(k * 512, (k + 1) * 512), kt == 0, kt == KT - 1)
                    i.then_inc(panel_used, 1)
                return n + 2

            def narrow_panel(n, outs):
                use(n)
                for b in range(TB):
                    for k in range(KT):
                        i = triple(outs[b], *xT(k, b), n, slice(k * 256, (k + 1) * 256), k == 0, k == KT - 1)
                i.then_inc(panel_used, 1)
                return n + 1

            def row_panel(n, lhs, first, last):
                use(n)
                for b in range(TB):
                    for k in range(2):
                        for h in range(2):
                            i = triple(bank[4 + 2 * b + h], *lhs(k, b), n, slice(k * 1024 + h * 512, k * 1024 + (h + 1) * 512),
                                       first and k == 0, last and k == 1)
                i.then_inc(panel_used, 1)
                return n + 1

            def transposed(h_, norm):
                pe.wait_ge(sem("h_ready"), norm + 1)
                for j in range(4):
                    for kk in range(2):
                        for b in range(TB):
                            k = 2 * j + kk
                            i = pe.transpose(bank[j][:, kk * SEQ + b * P:kk * SEQ + (b + 1) * P],
                                             h_[:, b, k * P:(k + 1) * P], ident)
                    i.then_inc(sem("hT_psum"), 1)

            pe.wait_ge(tab_loaded, 16)
            transposed(H, 0)
            pe.wait_ge(sem("xlo_ready"), 4)
            n = 0
            for c in range(3):
                if c == 2:
                    pe.wait_ge(sem("qkv_ready"), 1)
                n = wide_panels(n, [bank[4 + 2 * (c % 2) + b] for b in range(TB)])
            pe.wait_ge(sem("qkv_ready"), 3)
            for f in range(10):
                if f >= 4:
                    pe.wait_ge(sem("head_sb"), f - 3)
                for m in range(2):
                    col = (HEADS + 2 * f + m) * HD if f < 2 else (2 * f - 4 + m) * HD
                    for b in range(TB):
                        i = pe.transpose(bank[f % 4][0:HD, m * SEQ + b * P:m * SEQ + (b + 1) * P],
                                         qkv[:, b, col:col + HD], ident)
                i.then_inc(sem("head_psum"), 1)
            pe.wait_ge(sem("head_sb"), 10)
            pe.wait_ge(sem("pads_ready"), 1)

            def scores(n_):
                if n_ >= 2:
                    pe.wait_ge(sem("max_ready"), n_ - 1)
                for j in range(PAIRS):
                    o_ = bank[4 + 2 * (n_ % 2) + j // 4][:, j % 4 * P:(j % 4 + 1) * P]
                    i = pe.matmul(o_, qT[:, n_, 2 * j:2 * j + 2, :].rearrange("p h q -> p (h q)"),
                                  kT[:, j // 2, n_ * CHUNK:n_ * CHUNK + P], start=True, stop=True)
                i.then_inc(sem("score_psum"), 1)

            scores(0)
            for c in range(NCH):
                if c + 1 < NCH:
                    scores(c + 1)
                pe.wait_ge(sem("probs_ready"), c + 1)
                for j in range(PAIRS):
                    i = pe.transpose(bank[j // 4][:, j % 4 * P:(j % 4 + 1) * P], sc[:, c % 2, j * P:(j + 1) * P], ident)
                i.then_inc(sem("pT_psum"), 1)
                pe.wait_ge(sem("pT_ready"), c + 1)
                pe.wait_ge(sem("vsh_ready"), 1)
                if c >= 2:
                    pe.wait_ge(sem("oTlo_ready"), c - 1)
                for kv in range(KV_HEADS):
                    v_ = qkv[:, c // 2, QKV - 256 + kv * HD:QKV - 256 + (kv + 1) * HD] if c % 2 else \
                        vsh[:, c // 2, kv * HD:(kv + 1) * HD]
                    for r in range(2):
                        i = pe.matmul(bank[2 + c % 2][r * HD:(r + 1) * HD, kv * P:(kv + 1) * P], v_,
                                      pT[:, 2 * kv:2 * kv + 2, r * CHUNK:(r + 1) * CHUNK], start=True, stop=True)
                i.then_inc(sem("oT_psum"), 1)
            pe.wait_ge(sem("oTlo_ready"), NCH)
            for c in range(4):
                n = row_panel(n, lambda k, b: xT(2 * c + k, b), c == 0, c == 3)
            transposed(H, 1)
            pe.wait_ge(sem("xlo_ready"), 8)

            def hT(k, b):
                s_ = slice(k * SEQ + b * P, k * SEQ + (b + 1) * P)
                return hhi[:, s_], hlo[:, s_]

            for c in range(FCH + 1):
                if c < FCH:
                    n = narrow_panel(n, [bank[b][:, 0:256] for b in range(TB)])
                    n = narrow_panel(n, [bank[b][:, 256:512] for b in range(TB)])
                if c:
                    pe.wait_ge(sem("hlo_ready"), c)
                    n = row_panel(n, hT, c == 1, c == FCH)
                if c < FCH:
                    pe.wait_ge(sem("hid_ready"), c + 1)
                    for k in range(2):
                        for b in range(TB):
                            i = pe.transpose(bank[2][:, k * SEQ + b * P:k * SEQ + (b + 1) * P],
                                             hid[:, b * 256 + k * P:b * 256 + (k + 1) * P], ident)
                    i.then_inc(sem("hidT_psum"), 1)
            transposed(H, 2)
            pe.wait_ge(sem("xlo_ready"), 12)
            pe.wait_ge(loads, 112)
            pe.transpose(bank[6][:, 0:P], cwrow[:, :], ident).then_inc(sem("cw_psum"), 1)
            pe.wait_ge(sem("wba_lo"), 1)
            for b in range(TB):
                o_ = bank[4][:, b * 32:(b + 1) * 32]
                for k in range(KT):
                    a_, l_ = xT(k, b)
                    s_ = slice(k * 32, (k + 1) * 32)
                    pe.matmul(o_, a_, hhi[:, s_], start=k == 0, stop=False)
                    pe.matmul(o_, a_, hlo[:, s_], start=False, stop=False)
                    i = pe.matmul(o_, l_, hhi[:, s_], start=False, stop=k == KT - 1)
            i.then_inc(sem("ba_psum"), 1)
            pe.wait_ge(sem("gate_dve"), 2)
            for m, name in enumerate(("cum", "chunk", "first", "second")):
                i = pe.matmul(bank[5][:, m * 32:(m + 1) * 32], tb_(name), g32, start=True, stop=True)
            i.then_inc(sem("gsum_psum"), 1)
            pe.wait_ge(sem("gate_act"), 4)
            for g in range(GROUPS):
                if g:
                    pe.wait_ge(sem("o_done"), TB * g)
                n = narrow_panel(n, [bank[b][:, 0:256] for b in range(TB)])
                n = narrow_panel(n, [bank[b][:, 256:512] for b in range(TB)])
                n = wide_panels(n, [bank[2 + b] for b in range(TB)])
                n = wide_panels(n, [bank[4 + b] for b in range(TB)])
                pe.wait_ge(sem("prj_ready"), 2 * g + 2)
                for t in range(8):
                    for b in range(TB):
                        i = pe.transpose(bank[(6, 7, 0, 1)[t // 2]][:, t % 2 * SEQ + b * P:t % 2 * SEQ + (b + 1) * P],
                                         prj[:, t // 4, b, t % 4 * P:(t % 4 + 1) * P], ident)
                i.then_inc(sem("ch_psum"), 1)
                pe.wait_ge(sem("convs_ready"), g + 1)
                pe.wait_ge(sem("z_ready"), g + 1)
                for half in range(2):
                    for t in range(4):
                        for b in range(TB):
                            i = pe.transpose(bank[2 + 2 * half + b][:, t * P:(t + 1) * P],
                                             cvall[:, half * 4 + t, b * P:(b + 1) * P], ident)
                    i.then_inc(sem("back_psum"), 1)
                pe.wait_ge(sem("qkn_ready"), g + 1)
                for b in range(TB):
                    for t in range(4):
                        i = pe.transpose(bank[6 + b][:, t * P:(t + 1) * P], qk[:, 4 * b + t, :], ident)
                i.then_inc(sem("qkT_psum"), 1)
                for b in range(TB):
                    i = pe.matmul(bank[b], tb_("ones"), gm[:, 4 * b:4 * b + 4, :], start=True, stop=True)
                i.then_inc(sem("R_psum"), 1)
                pe.wait_ge(sem("qkT_ready"), g + 1)
                for b in range(TB):
                    for kh in range(2):
                        kq = qkT[:, 4 * b:4 * b + 4, :].rearrange("p (m k) f -> p k m f", m=2)[:, kh]
                        i = pe.matmul(bank[2 + b][:, kh * 256:(kh + 1) * 256], qkT[:, 4 * b + 2 + kh, :], kq,
                                      start=True, stop=True)
                i.then_inc(sem("kk_psum"), 1)
                pe.wait_ge(sem("scaled"), 3 * g + 3)
                pe.wait_ge(sem("vb_ready"), g + 1)
                for m in range(8):
                    i = pe.transpose(bank[4 + m // 4][:, m % 4 * P:(m % 4 + 1) * P], qdec[:, m, :], ident)
                i.then_inc(sem("qdT_psum"), 1)
                pe.wait_ge(sem("T0_ready"), g + 1)
                for b in range(TB):
                    for h in range(GH):
                        i = pe.transpose(bank[b][:, h * P:(h + 1) * P], T[:, 4 * b + h, :], ident)
                    i.then_inc(sem("TT0_psum"), 1)
                pe.wait_ge(sem("qdT_ready"), g + 1)
                for lv in range(1, 6):
                    u = g * 5 + lv - 1
                    o = off0 if lv % 2 else off1
                    pe.wait_ge(sem("off_ready"), u + 1)
                    for b in range(TB):
                        if lv == 1:
                            pe.wait_ge(sem("TT0_ready"), 2 * g + b + 1)
                        else:
                            pe.wait_ge(sem("TT_ready"), 2 * (u - 1) + b + 1)
                        for h in range(GH):
                            i = pe.matmul(bank[2 + b][:, h * P:(h + 1) * P], o[:, 4 * b + h, :], TT[:, 4 * b + h, :],
                                          start=True, stop=True)
                        i.then_inc(sem("P_psum"), 1)
                    for b in range(TB):
                        pe.wait_ge(sem("P_ready"), 2 * u + b + 1)
                        if lv > 1:
                            pe.wait_ge(sem("T_ready"), 2 * (g * 4 + lv - 2) + b + 1)
                        for h in range(GH):
                            i = pe.matmul(bank[4 + b][:, h * P:(h + 1) * P], T[:, 4 * b + h, :], Pm[:, 4 * b + h, :],
                                          start=True, stop=True)
                        i.then_inc(sem("dTT_psum"), 1)
                    if lv < 5:
                        for b in range(TB):
                            pe.wait_ge(sem("TT_ready"), 2 * u + b + 1)
                            for h in range(GH):
                                i = pe.transpose(bank[b][:, h * P:(h + 1) * P], TT[:, 4 * b + h, :], ident)
                            i.then_inc(sem("T_psum"), 1)
                pe.wait_ge(sem("TT_ready"), 2 * (g * 5 + 5))
                for m in range(8):
                    i = pe.matmul(bank[4 + m // 4][:, m % 4 * P:(m % 4 + 1) * P], kbe[:, m, :], TT[:, m, :], start=True, stop=True)
                i.then_inc(sem("wT_psum"), 1)
                for c in range(NCH):
                    b, r0 = c // 2, c % 2 * CHUNK
                    rr = slice(r0, r0 + CHUNK)
                    if c == 0:
                        pe.wait_ge(sem("wT_ready"), g + 1)
                    else:
                        pe.wait_ge(sem("S_ready"), g * (NCH - 1) + c)
                    for h in range(GH):
                        o_ = bank[0][rr, h * P:(h + 1) * P]
                        m = 4 * b + h
                        i = pe.matmul(o_, TT[:, m, rr], vb[:, m, :], start=True, stop=c == 0)
                        if c:
                            i = pe.matmul(o_, wT[:, m, rr], S[:, h, :], start=False, stop=True)
                    i.then_inc(sem("v_psum"), 1)
                    pe.wait_ge(sem("v_ready"), g * NCH + c + 1)
                    for h in range(GH):
                        o_ = bank[6 + b][rr, h * P:(h + 1) * P]
                        m = 4 * b + h
                        i = pe.matmul(o_, attnT[rr, m, rr], vnew[rr, h, :], start=True, stop=c == 0)
                        if c:
                            i = pe.matmul(o_, qdecT[:, m, rr], S[:, h, :], start=False, stop=True)
                    if c % 2:
                        i.then_inc(sem("o_psum"), 1)
                    if c < NCH - 1:
                        for h in range(GH):
                            i = pe.matmul(bank[1][:, h * P:(h + 1) * P], ktail[rr, 4 * b + h, :], vnew[rr, h, :],
                                          start=True, stop=True)
                        i.then_inc(sem("s_psum"), 1)
            pe.wait_ge(sem("o_done"), TB * GROUPS)
            for f in range(8 + 1):
                if f < 8:
                    if f >= 4:
                        pe.wait_ge(sem("onlo_ready"), f - 3)
                    for kk in range(2):
                        for b in range(TB):
                            k = 2 * f + kk
                            i = pe.transpose(bank[f % 4][:, kk * SEQ + b * P:kk * SEQ + (b + 1) * P],
                                             oall[:, b, k * P:(k + 1) * P], ident)
                    i.then_inc(sem("on_psum"), 1)
                if f:
                    pe.wait_ge(sem("onlo_ready"), f)
                    n = row_panel(n, lambda k, b: xT((2 * (f - 1) + k) % 8, b), f == 1, f == 8)
            transposed(H3, 3)
            pe.wait_ge(sem("hTf_ready"), 4)
            for b in range(TB):
                for k in range(KT):
                    i = pe.matmul(bank[4][:, b * NE:(b + 1) * NE], hTf[:, k, b * P:(b + 1) * P], wr[:, k * NE:(k + 1) * NE],
                                  start=k == 0, stop=k == KT - 1)
            i.then_inc(sem("logit_psum"), 1)
            pe.wait_ge(sem("route_dve"), 2)
            pe.matmul(bank[5][:, 0:NE], tb_("tri"), msk[:, 0:NE], start=True, stop=True)
            pe.matmul(bank[5][:, NE:2 * NE], tb_("ones"), msk[:, 0:NE], start=True, stop=False)
            pe.matmul(bank[5][:, NE:2 * NE], tb_("tri"), msk[:, NE:2 * NE], start=False, stop=True)
            pe.matmul(bank[5][:, 2 * NE:3 * NE], tb_("ones"), msk[:, 0:NE], start=True, stop=False)
            pe.matmul(bank[5][:, 2 * NE:3 * NE], tb_("ones"), msk[:, NE:2 * NE], start=False, stop=True)\
                .then_inc(sem("rank_psum"), 1)
            pe.wait_ge(sem("h2lo_ready"), 1)
            pe.wait_ge(sem("npass_ready"), 1)
            passes = pe.value_load(npass[0:1, 0:1], min_val=1, max_val=2)

            def gxT(k):
                return xhi[:, k * P:(k + 1) * P], xlo[:, k * P:(k + 1) * P]

            def gate_up(it, local, more, u):
                for m in range(4):
                    nn = P_MOE + local + m
                    pe.wait_ge(lo_ready, it * EP + more * 6 + (nn + 1))
                    for k in range(4):
                        kt = m % 2 * 4 + k
                        i = triple(bank[m // 2], *gxT(kt), nn, slice(k * 512, (k + 1) * 512), kt == 0, kt == KT - 1)
                    i.then_inc(panel_used, 1)

            def down(it, local, more, u, first, last):
                pe.wait_ge(sem("ehlo_ready"), u + 1)
                for m in range(2):
                    nn = P_MOE + local + m
                    pe.wait_ge(lo_ready, it * EP + more * 6 + (nn + 1))
                    for k in range(2):
                        s_ = slice((2 * m + k) * P, (2 * m + k + 1) * P)
                        for h in range(2):
                            i = triple(bank[3 + h], hhi[:, s_], hlo[:, s_], nn, slice(k * 1024 + h * 512, k * 1024 + (h + 1) * 512),
                                       first and m == 0 and k == 0, last and m == 1 and k == 1)
                    i.then_inc(panel_used, 1)

            def hidden_T(u):
                pe.wait_ge(sem("ehid_ready"), u + 1)
                for k in range(4):
                    i = pe.transpose(bank[2][:, k * P:(k + 1) * P], hid[:, k * P:(k + 1) * P], ident)
                i.then_inc(sem("ehT_psum"), 1)

            with pe.Fori(0, passes) as q:
                with pe.Fori(0, NE) as e:
                    it = q * NE + e
                    pe.wait_ge(sem("sel_ready"), it + 1)
                    pe.wait_ge(sem("acc_added"), it * 4 + 1)
                    for b in range(TB):
                        i = pe.transpose(bank[5][:, b * P:(b + 1) * P], sel[:, b, :].bitcast(F32), ident)
                    i.then_inc(sem("selT_psum"), 1)
                    for h in range(2):
                        for k in range(4):
                            o_ = bank[6 + h][:, k * P:(k + 1) * P]
                            d_ = slice((4 * h + k) * P, (4 * h + k + 1) * P)
                            for b in range(TB):
                                pe.matmul(o_, h2hi[:, b, d_], sel[:, b, :], start=b == 0, stop=False)
                                i = pe.matmul(o_, h2lo[:, b, d_], sel[:, b, :], start=False, stop=b == TB - 1)
                        i.then_inc(sem("gath_psum"), 1)
                    pe.wait_ge(sem("gxlo_ready"), it * 2 + 2)
                    u0 = it * ECH
                    gate_up(it, 0, 0, u0)
                    hidden_T(u0)
                    gate_up(it, 4, 0, u0 + 1)
                    down(it, 8, 0, u0, True, False)
                    hidden_T(u0 + 1)
                    with pe.Fori(2, ECH) as c:
                        gate_up(it, 10, c - 2, u0 + c)
                        down(it, 14, c - 2, u0 + (c - 1), False, False)
                        hidden_T(u0 + c)
                    down(it, EP - 2, 0, u0 + (ECH - 1), False, True)
                    pe.wait_ge(sem("selT_ready"), it + 1)
                    pe.wait_ge(sem("ylo_ready"), it + 1)
                    for k in range(4):
                        b, h = divmod(k, 2)
                        if k >= 2:
                            pe.wait_ge(sem("acc_added"), it * 4 + k)
                        s_, t_ = slice(h * 512, (h + 1) * 512), selT[:, b * P:(b + 1) * P]
                        pe.matmul(bank[5 + k % 2], t_, yhi[:, s_], start=True, stop=False)
                        pe.matmul(bank[5 + k % 2], t_, ylo[:, s_], start=False, stop=True).then_inc(sem("comb_psum"), 1)


_INS = ["x", "norm_g", "final_norm_g", "attn_w_qkv", "attn_b_qkv", "attn_sinks", "attn_w_o", "dn_w_in", "dn_conv_w",
        "dn_a_log", "dn_dt_bias", "dn_norm_g", "dn_w_o", "ffn_w_gate", "ffn_w_up", "ffn_w_down", "moe_w_router",
        "moe_w_gate", "moe_w_up", "moe_w_down"]
_SINGLE = ["attn_w_qkv", "attn_w_o", "dn_w_in", "dn_w_o", "ffn_w_gate", "ffn_w_up", "ffn_w_down",
           "moe_w_gate", "moe_w_up", "moe_w_down"]


def kernel(**inputs):
    import concourse.bacc as _bacc
    from concourse.bass_utils import run_bass_kernel_spmd as _run

    nc = _bacc.Bacc("TRN2", target_bir_lowering=False, num_devices=1)
    arrays, args = {}, []

    def given(name, a):
        arrays[name] = a
        return nc.dram_tensor(name, a.shape, mybir.dt.from_np(a.dtype), kind="ExternalInput").ap()

    for name in _INS:
        a = given(f"in_{name}_dram", np.ascontiguousarray(inputs[name]))
        args.append(a[0] if name in _SINGLE else a)
    args.append(given("table_dram", table()))
    args.append(given("alibi_dram", alibi()))
    args.append(nc.dram_tensor("out_0_dram", (1, SEQ, D), F32, kind="ExternalOutput").ap())
    trunk(nc, *args)
    r = _run(nc, [arrays], core_ids=[0])
    return r.results[0]["out_0_dram"]
```

```python
from contextlib import ExitStack

import numpy as np

import concourse.bass as bass
from concourse import mybir

ALU = mybir.AluOpType
ACT = mybir.ActivationFunctionType
F32 = mybir.dt.float32
F32R = mybir.dt.float32r
I32 = mybir.dt.int32
U32 = mybir.dt.uint32
AX_X = mybir.AxisListType.X

P = 128
SEQ = 256
TB = SEQ // P
D = 1024
KT = D // P
EPS = 1e-6
CHUNK = 64
NCH = SEQ // CHUNK
HEADS, KV_HEADS, HD = 16, 4, 64
QKV = (HEADS + 2 * KV_HEADS) * HD
PAIRS = HEADS // 2
DFF = 2816
QK_DIM, V_DIM, BH = 1024, 2048, 128
VH = 16
GROUPS = 4
GH = VH // GROUPS
IN_DIM = 2 * QK_DIM + 2 * V_DIM + 2 * VH
NE = 8
FFE = 3584
ECH = FFE // 512
BIG = 1e30

PANEL = 2048
RAW, SPLIT = 6, 3

TABLE = {}


def table():
    i, j = np.arange(P)[:, None], np.arange(P)[None, :]
    same = i // CHUNK == j // CHUNK
    parts = {
        "ident": i == j,
        "cum": same & (i <= j),
        "chunk": same,
        "first": (i < CHUNK) & (j >= 0),
        "second": (i >= CHUNK) & (j >= 0),
        "off_strict": np.where(same & (i > j), 0.0, BIG),
        "off_upper": np.where(same & (i <= j), 0.0, BIG),
        "tri": i <= j,
        "ones": (i >= 0) & (j >= 0),
        "iota": j + 0 * i,
    }
    for n in range(6):
        s = 1 << n
        parts[f"level{n}"] = (i // (2 * s) == j // (2 * s)) & (i // s % 2 == 1) & (j // s % 2 == 0)
    at, out = 0, []
    for name, a in parts.items():
        TABLE[name] = at
        at += P
        out.append(a.astype(np.float32))
    return np.ascontiguousarray(np.concatenate(out, axis=1))


def alibi():
    slope = np.exp2(-8.0 * np.arange(1, HEADS + 1, dtype=np.float32) / HEADS)
    dist = np.abs(np.arange(CHUNK)[:, None] + CHUNK - np.arange(2 * CHUNK)[None, :]).astype(np.float32)
    a = -(slope.reshape(PAIRS, 2, 1, 1) * dist).transpose(1, 2, 0, 3).reshape(P, PAIRS, 2 * CHUNK)
    first = a.copy()
    first[:, :, :CHUNK] = -BIG
    return np.ascontiguousarray(np.stack([first, a]).astype(np.float32).reshape(2, P, PAIRS * P))


def trunk(nc, x, norm_g, final_norm_g, w_qkv, b_qkv, sinks, w_o, w_in, conv_w, a_log, dt_bias, dn_norm_g,
          dn_w_o, f_gate, f_up, f_down, w_router, e_gate, e_up, e_down, tab, ali, out):
    sems = {}
    psum = [nc.alloc_psum_tensor(f"bank{n}", [P, 512], F32) for n in range(8)]
    bank = [b[:, :] for b in psum]

    base = (nc.sbuf_base + 63) // 64 * 64
    KB = 1024

    def at(name, n, kb, dt=F32, parts=P):
        return nc.alloc_sbuf_tensor_at(name, [parts, n], dt, offset=base + int(kb * KB))

    raw = at("raw", RAW * PANEL, 0)
    whi = at("whi", SPLIT * PANEL, 48, F32R)
    wlo = at("wlo", SPLIT * PANEL, 72, F32R)
    xhi = at("xhi", 2048, 96, F32R)
    xlo = at("xlo", 2048, 104, F32R)
    X = at("X", TB * D, 112)[:, :].rearrange("p (b d) -> p b d", b=TB)
    tabs = at("tabs", 16 * P, 120)
    par = at("par", 964, 128)
    S = at("S", GH * BH, 131.875)[:, :].rearrange("p (h d) -> p h d", h=GH)
    W0 = 133.875
    squares = at("squares", TB * D, W0 + 4)[:, :].rearrange("p (b d) -> p b d", b=TB)
    qkv = at("qkv", TB * QKV, W0 + 12)[:, :].rearrange("p (b d) -> p b d", b=TB)
    qT = at("qT", HEADS * SEQ, W0 + 24)[0:HD, :].rearrange("p (n h q) -> p n h q", n=NCH, h=HEADS)
    kT = at("kT", KV_HEADS * (CHUNK + SEQ), W0 + 40)[0:HD, :].rearrange("p (h t) -> p h t", h=KV_HEADS)
    abias = at("abias", 2 * PAIRS * P, W0 + 45)[:, :].rearrange("p (n f) -> p n f", n=2)
    bqkv = at("bqkv", QKV, W0 + 53)
    sc = at("sc", 2 * PAIRS * P, W0 + 59)[:, :].rearrange("p (n f) -> p n f", n=2)
    pT = at("pT", PAIRS * P, W0 + 67)[:, :].rearrange("p (j c) -> p j c", j=PAIRS)
    vsh = at("vsh", 2 * 256, W0 + 71)[:, :].rearrange("p (n f) -> p n f", n=2)
    hhi = at("hhi", 512, W0 + 16, F32R)
    hlo = at("hlo", 512, W0 + 18, F32R)
    sil = at("sil", 512, W0 + 30)
    hid = at("hid", 512, W0 + 32)
    def eight(name, kb):
        return at(name, 8 * P, W0 + kb)[:, :].rearrange("p (n f) -> p n f", n=8)
    kbe, qdec, off0 = eight("kbe", 0), eight("qdec", 4), eight("off0", 8)
    oall = at("oall", TB * V_DIM, W0 + 12)[:, :].rearrange("p (b d) -> p b d", b=TB)
    prj_v = at("prj_v", TB * 512, W0 + 4)[:, :].rearrange("p (b d) -> p b d", b=TB)
    attnT, wT = eight("attnT", 28), eight("wT", 32)
    cvall = at("cvall", 8 * SEQ, W0 + 36)[:, :].rearrange("p (n f) -> p n f", n=8)
    qdecT, ktail = eight("qdecT", 36), eight("ktail", 40)
    qk = eight("qk", 44)
    vb = eight("vb", 48)
    qkT, off1 = eight("qkT", 52), eight("off1", 52)
    A = eight("A", 56)
    dT, T = eight("dT", 60), eight("T", 60)
    dA, TT = eight("dA", 64), eight("TT", 64)
    gm, Pm = eight("gm", 68), eight("Pm", 68)
    vnew = at("vnew", GH * BH, W0 + 0)[:, :].rearrange("p (h d) -> p h d", h=GH)
    osq = at("osq", 512, W0 + 8)
    otmp = at("otmp", 512, W0 + 10)
    h2hi = at("h2hi", TB * D, W0 + 0, F32R)[:, :].rearrange("p (b d) -> p b d", b=TB)
    h2lo = at("h2lo", TB * D, W0 + 8, F32R)[:, :].rearrange("p (b d) -> p b d", b=TB)
    sel = at("sel", TB * P, W0 + 20, F32R)[:, :].rearrange("p (b s) -> p b s", b=TB)
    selT = at("selT", TB * P, W0 + 21, F32R)
    yhi = at("yhi", D, W0 + 22, F32R)
    ylo = at("ylo", D, W0 + 26, F32R)
    hTf = at("hTf", KT * SEQ, W0 + 34)[:, :].rearrange("p (k t) -> p k t", k=KT)
    gain3 = at("gain3", D, W0 + 42)
    H3 = at("H3", TB * D, W0 + 46)[:, :].rearrange("p (b d) -> p b d", b=TB)
    small_at = [0]

    def small(n):
        a = par[:, small_at[0]:small_at[0] + n]
        small_at[0] += n
        return a
    ms, rs = small(2), small(2)
    halfneg = small(8)
    sink8 = small(8)
    mx, nm, es, ssum, rsum = ([small(8), small(8)] for _ in range(5))
    gcol = small(4 * KT)
    ba = small(TB * 2 * VH)
    sink16 = small(HEADS)
    convw = small(P)
    convw_v = convw.rearrange("p (w t) -> p w t", w=4)
    alog, dtb = small(VH), small(VH)
    wr = small(KT * NE)
    g32, beta, gc, egc, ebeta, etail, sa, sb_ = (small(2 * VH) for _ in range(8))
    egl = small(4 * VH)
    r8, ss8 = small(8), small(8)
    lg, top, oh1, oh2, tmp8, msk = (small(TB * NE) for _ in range(6))
    pos, cmb = (small(TB * (NE + 1)).rearrange("p (b e) -> p b e", b=TB) for _ in range(2))
    topi = small(TB * NE)
    gt, e2, cnt = small(4), small(4), small(1)
    assert small_at[0] <= 964
    wba = at("wba", KT * 2 * VH, W0 + 72.0 - 1)
    npass = at("npass", 1, 131.8125, I32)
    ngain = at("ngain", BH, W0 + 72)
    cwrow = at("cwrow", P, 131.875)

    grow = at("grow", P, 132.875, parts=4 * KT)

    def tb_(name):
        return tabs[:, TABLE[name]:TABLE[name] + P]

    ident = tb_("ident")

    with ExitStack() as ctx:
        def sem(name):
            if name not in sems:
                sems[name] = ctx.enter_context(nc.semaphore(name))
            return sems[name]

        landed = [sem(f"panel_landed{n}") for n in range(RAW)]
        hi_ready, lo_ready, panel_used = sem("hi_ready"), sem("lo_ready"), sem("panel_used")
        loads = sem("params_loaded")
        x_loaded, gain_loaded, tab_loaded = sem("x_loaded"), sem("gain_loaded"), sem("tab_loaded")
        phase_b_params = sem("phase_b_params")

        panels = []

        def wide(w, n0):
            for half in range(2):
                panels.append((w[half * 512:half * 512 + 512, n0:n0 + 512].rearrange("(k p) n -> p k n", p=P), 4))

        def narrow(w, n0):
            panels.append((w[:, n0:n0 + 256].rearrange("(k p) n -> p k n", p=P), 8))

        def rows(w, k0):
            panels.append((w[k0:k0 + 256, :].rearrange("(k p) n -> p k n", p=P), 2))

        for c in range(3):
            wide(w_qkv, c * 512)
        P_WO = len(panels)
        for c in range(4):
            rows(w_o, c * 256)
        P_FFN = len(panels)
        FCH = DFF // 256
        for c in range(FCH + 1):
            if c < FCH:
                narrow(f_gate, c * 256)
                narrow(f_up, c * 256)
            if c:
                rows(f_down, (c - 1) * 256)
        P_IN = len(panels)
        for g in range(GROUPS):
            narrow(w_in, g * 256)
            narrow(w_in, QK_DIM + g * 256)
            wide(w_in, 2 * QK_DIM + g * 512)
            wide(w_in, 2 * QK_DIM + V_DIM + g * 512)
        P_DNO = len(panels)
        for c in range(V_DIM // 256):
            rows(dn_w_o, c * 256)
        P_MOE = len(panels)
        EP = 6 * ECH
        assert EP % RAW == 0 and EP % SPLIT == 0

        def slot(t, n, ring):
            return t[:, (n % ring) * PANEL:(n % ring + 1) * PANEL]

        class Split:
            def __init__(self, one):
                self.one, self.n = one, 0

            def upto(self, n):
                while self.n <= min(n, P_MOE - 1):
                    self.one(self.n, self.n)
                    self.n += 1

        def chunk_panel(sp, it, c, i, src):
            sp.wait_ge(lo_ready, it * EP + c * 6 + (P_MOE + 10 - 12 + i - RAW + 1))
            n = P_MOE + 10 + i
            sp.dma_start(slot(raw, n, RAW).rearrange("p (k n) -> p k n", k=src.shape[1] // P),
                         src.rearrange("a (k p) n -> p (a k) n", p=P)).then_inc(landed[n % RAW], 16)

        SPLIT_AFTER = (3, 4, 5, 6, 6, 7)

        def conv_src(t):
            return bank[(4, 5, 2, 3)[t // 2]][:, t % 2 * SEQ:(t % 2 + 1) * SEQ]

        def tap(g, t, w):
            tile = (2 * g + t) if t < 2 else (8 + 2 * g + t - 2) if t < 4 else (16 + 4 * g + t - 4)
            return convw_v[:, w, tile:tile + 1]

        def group_part(g):
            return oall[:, :, g * 512:(g + 1) * 512]

        block = ctx.enter_context(nc.Block())

        @block.sync
        def _(sp):
            sp.dma_start(X, x[0].rearrange("(b p) d -> p b d", p=P)).then_inc(x_loaded, 16)
            sp.dma_start(tabs[:, :], tab).then_inc(tab_loaded, 16)
            sp.dma_start(grow[:, :], norm_g.rearrange("l n (k p) -> (l n k) p", p=P)).then_inc(sem("rows_loaded"), 16)
            sp.dma_start(cwrow[:, :], conv_w[0].rearrange("w (t c) -> (w t) c", c=P)).then_inc(sem("rows_loaded"), 16)

            def panel(n, src, free):
                if free is not None:
                    sp.wait_ge(lo_ready, free)
                k = src.shape[1]
                sp.dma_start(slot(raw, n, RAW).rearrange("p (k n) -> p k n", k=k), src).then_inc(landed[n % RAW], 16)

            def upto(n0, n1):
                for n in range(n0, n1):
                    panel(n, panels[n][0], n - RAW + 1 if n >= RAW else None)

            upto(0, 2)
            sp.dma_start(bqkv[:, :], b_qkv.partition_broadcast(P)[:, 0]).then_inc(loads, 16)
            sp.dma_start(abias, ali.rearrange("n p f -> p n f")).then_inc(loads, 16)
            sp.dma_start(sink16, sinks.partition_broadcast(P)[:, 0]).then_inc(loads, 16)
            sp.dma_start(alog, a_log.partition_broadcast(P)[:, 0]).then_inc(loads, 16)
            sp.dma_start(dtb, dt_bias.partition_broadcast(P)[:, 0]).then_inc(loads, 16)
            sp.dma_start(wr.rearrange("p (k e) -> p k e", k=KT), w_router[0].rearrange("(k p) e -> p k e", p=P)).then_inc(loads, 16)
            upto(2, P_WO)
            upto(P_WO, P_FFN + 3)
            sp.wait_ge(sem("x_ready"), 2)
            sp.dma_start(wba[:, :].rearrange("p (k n) -> p k n", k=KT),
                         w_in[:, IN_DIM - 2 * VH:].rearrange("(k p) n -> p k n", p=P)).then_inc(phase_b_params, 16)
            sp.dma_start(ngain[:, :], dn_norm_g.partition_broadcast(P)[:, 0]).then_inc(phase_b_params, 16)
            upto(P_FFN + 3, P_DNO)
            upto(P_DNO, P_DNO + 3)
            sp.wait_ge(sem("o_done"), TB * GROUPS)
            sp.dma_start(gain3[:, :], norm_g[1, 1:2, :].partition_broadcast(P)[:, 0]).then_inc(gain_loaded, 16)
            upto(P_DNO + 3, P_MOE)

            def expert_panel(e, it, local, src):
                sp.wait_ge(lo_ready, it * EP + (P_MOE + local - RAW + 1))
                n = P_MOE + local
                k = src.shape[1]
                sp.dma_start(slot(raw, n, RAW).rearrange("p (k n) -> p k n", k=k), src).then_inc(landed[n % RAW], 16)

            def up_panels(e, it, local, c):
                for w in (e_gate, e_up):
                    for half in range(2):
                        src = w[bass.ds(e, 1), half * 512:half * 512 + 512, bass.ds(c * 512, 512)]
                        expert_panel(e, it, local, src.rearrange("a (k p) n -> p (a k) n", p=P))
                        local = local + 1

            def down_panels(e, it, local, c):
                rows_ = e_down.rearrange("e r n -> (e r) n")
                for half in range(2):
                    src = rows_[bass.ds(e * FFE + (c * 512 + half * 256), 256), :].unsqueeze(0)
                    expert_panel(e, it, local + half, src.rearrange("a (k p) n -> p (a k) n", p=P))

            def head(e, it):
                up_panels(e, it, 0, 0)
                for i in range(2):
                    expert_panel(e, it, 4 + i, e_gate[bass.ds(e, 1), i * 512:i * 512 + 512, 512:1024]
                                 .rearrange("a (k p) n -> p (a k) n", p=P))

            def body(e, it):
                for i in range(2):
                    expert_panel(e, it, 6 + i, e_up[bass.ds(e, 1), i * 512:i * 512 + 512, 512:1024]
                                 .rearrange("a (k p) n -> p (a k) n", p=P))
                down_panels(e, it, 8, 0)
                with sp.Fori(2, ECH) as c:
                    for i, w in enumerate((e_gate, e_gate, e_up, e_up)):
                        chunk_panel(sp, it, c, i, w[bass.ds(e, 1), i % 2 * 512:i % 2 * 512 + 512, bass.ds(c * 512, 512)])
                    for i in range(2):
                        chunk_panel(sp, it, c, 4 + i, e_down[bass.ds(e, 1), bass.ds(c * 512 + (i * 256 - 512), 256), :])
                down_panels(e, it, EP - 2, ECH - 1)

            head(0, 0)
            sp.wait_ge(sem("npass_ready"), 1)
            passes = sp.value_load(npass[0:1, 0:1], min_val=1, max_val=2)
            turns = passes * NE
            with sp.Fori(0, turns - 1) as it:
                e, following = sp.snap(it % NE), sp.snap((it + 1) % NE)
                body(e, it)
                head(following, it + 1)
            body(NE - 1, turns - 1)
            sp.wait_ge(sem("h_ready"), 1)
            sp.dma_start(gain3[:, :], final_norm_g.rearrange("(a d) -> a d", a=1).partition_broadcast(P)[:, 0]).then_inc(gain_loaded, 16)
            sp.wait_ge(sem("h_ready"), 2)
            sp.dma_start(out[0].rearrange("(b p) d -> p b d", p=P), H3).then_inc(sem("out_stored"), 16)
            sp.wait_ge(sem("out_stored"), 16)

        @block.gpsimd
        def _(pool):
            pool.memset(halfneg, -0.5).then_inc(sem("pool_const"), 1)
            pool.wait_ge(sem("pool_const"), 1)

            def rsqrt(dst, src, n, asked, count, scale):
                pool.wait_ge(sem(asked), count)
                pool.tensor_scalar(src, src, scale, EPS, ALU.mult, ALU.add).then_inc(sem("mean_ready"), 1)
                powers[0] += 1
                pool.wait_ge(sem("mean_ready"), powers[0])
                pool.tensor_tensor(dst, src, halfneg[:, 0:n], ALU.pow).then_inc(sem("rs_ready"), 1)

            powers = [0]

            def spread_g(g):
                for b in range(TB):
                    f_ = g32[:, b * VH + g * GH:b * VH + g * GH + GH].unsqueeze(2).broadcast_to([P, GH, P])
                    c_ = tb_("cum").unsqueeze(1).broadcast_to([P, GH, P])
                    i = pool.tensor_tensor(gm[:, 4 * b:4 * b + 4, :], c_, f_, ALU.mult)
                i.then_inc(sem("gm_ready"), 1)

            for m in range(3):
                rsqrt(rs, ms, 2, "ms_ready", m + 1, 1.0 / D)
            pool.wait_ge(sem("gate_dve"), 2)
            spread_g(0)
            for g in range(GROUPS):
                rsqrt(r8, ss8, 8, "sq_ready", 3 * g + 1, 1.0)
                pool.wait_ge(sem("qkn_ready"), g + 1)
                for src0, dst, fac in ((0, qdec, egc), (2, kbe, ebeta), (2, ktail, etail)):
                    for b in range(TB):
                        s_ = qk[:, 4 * b + src0:4 * b + src0 + 2, :].unsqueeze(2).broadcast_to([P, 2, 2, P])
                        f_ = fac[:, b * VH + g * GH:b * VH + g * GH + GH].rearrange("p (k r) -> p k r", r=2)
                        f_ = f_.unsqueeze(3).broadcast_to([P, 2, 2, P])
                        d_ = dst[:, 4 * b:4 * b + 4, :].rearrange("p (k r) f -> p k r f", r=2)
                        i = pool.tensor_tensor(d_, s_, f_, ALU.mult)
                    i.then_inc(sem("scaled"), 1)
                pool.wait_ge(sem("A_ready"), g + 1)
                for lv in range(1, 6):
                    o = off0 if lv % 2 else off1
                    if lv >= 3:
                        pool.wait_ge(sem("P_psum"), (g * 5 + lv - 2) * 2)
                    m_ = tb_(f"level{lv}").unsqueeze(1).broadcast_to([P, 8, P])
                    pool.tensor_tensor(o, A, m_, ALU.mult).then_inc(sem("off_ready"), 1)
                pool.wait_ge(sem("z_ready"), g + 1)
                for b in range(TB):
                    z_ = oall[:, b, g * 512:(g + 1) * 512].rearrange("p (h d) -> p h d", h=GH)
                    i = pool.tensor_tensor(z_, z_, ngain[:, :].unsqueeze(1).broadcast_to([P, GH, BH]), ALU.mult)
                i.then_inc(sem("zg_ready"), 1)
                if g + 1 < GROUPS:
                    pool.wait_ge(sem("dTT_psum"), 2 * (5 * g + 5))
                    spread_g(g + 1)
                for b in range(TB):
                    rsqrt(r8[:, 0:4], ss8[:, 0:4], 4, "sq_ready", 3 * g + 2 + b, 1.0 / BH)
            for m in range(2):
                rsqrt(rs, ms, 2, "ms_ready", 4 + m, 1.0 / D)

        @block.scalar
        def _(act):
            chain = [0]

            def link(i):
                chain[0] += 1
                i.then_inc(sem("act_chain"), 1)
                act.wait_ge(sem("act_chain"), chain[0])

            def hi(n, v):
                act.wait_ge(landed[n % RAW], 16 * (v // RAW + 1))
                if v >= SPLIT:
                    act.wait_ge(panel_used, v - SPLIT + 1)
                act.copy(slot(whi, n, SPLIT), slot(raw, n, RAW)).then_inc(hi_ready, 1)

            hi_panels = Split(hi)

            def split_hi(norm):
                for j in range(4):
                    act.wait_ge(sem("hT_psum"), 4 * norm + j + 1)
                    for k in range(2 * j, 2 * j + 2):
                        i = act.activation(xhi[:, k * SEQ:(k + 1) * SEQ], bank[j][:, k % 2 * SEQ:(k % 2 + 1) * SEQ],
                                           ACT.Copy, scale=gcol[:, norm * KT + k:norm * KT + k + 1])
                    i.then_inc(sem("xhi_ready"), 1)
                for b in range(TB):
                    i = act.activation(squares[:, b, :], X[:, b, :], ACT.Square, accum_out=ms[:, b:b + 1])
                i.then_inc(sem("ms_ready"), 1)

            act.wait_ge(sem("gcol_ready"), 1)
            act.wait_ge(x_loaded, 16)
            split_hi(0)
            hi_panels.upto(P_WO - 1)
            act.wait_ge(sem("qkv_ready"), 3)
            act.copy(vsh[HD:P, 0, :], qkv[0:HD, 0, QKV - 256:])
            act.copy(vsh[0:HD, 1, :], qkv[HD:P, 0, QKV - 256:])
            act.copy(vsh[HD:P, 1, :], qkv[0:HD, 1, QKV - 256:]).then_inc(sem("vsh_ready"), 1)
            for f in range(10):
                act.wait_ge(sem("head_psum"), f + 1)
                if f < 2:
                    src = bank[f % 4][0:HD, :].rearrange("p (h t) -> p h t", h=2)
                    dst = kT[:, 2 * f:2 * f + 2, CHUNK:]
                else:
                    src = bank[f % 4][0:HD, :].rearrange("p (h n q) -> p h n q", h=2, n=NCH)
                    dst = qT[:, :, 2 * f - 4:2 * f - 2, :].rearrange("p n h q -> p h n q")
                act.copy(dst, src).then_inc(sem("head_sb"), 1)
            hi_panels.upto(P_WO + 2)

            def exps(n):
                act.wait_ge(sem("max_ready"), n + 1)
                act.activation(es[n % 2], es[n % 2], ACT.Exp)
                for j in range(PAIRS):
                    s_ = sc[:, n % 2, j * P:(j + 1) * P]
                    i = act.activation(s_, s_, ACT.Exp, bias=nm[n % 2][:, j:j + 1], scale=1.0, accum_out=ssum[n % 2][:, j:j + 1])
                i.then_inc(sem("exp_ready"), 1)

            def probs_T(n):
                act.wait_ge(sem("pT_psum"), n + 1)
                if n:
                    act.wait_ge(sem("oT_psum"), n)
                for h in range(2):
                    i = act.copy(pT[:, 4 * h:4 * h + 4, :], bank[h].rearrange("p (j c) -> p j c", j=4))
                i.then_inc(sem("pT_ready"), 1)

            def attended_hi(n):
                act.wait_ge(sem("oT_psum"), n + 1)
                o_ = bank[2 + n % 2].rearrange("p (j t) -> p j t", j=PAIRS)
                act.copy(xhi[:, :].rearrange("p (j t) -> p j t", j=PAIRS)[:, :, n * CHUNK:(n + 1) * CHUNK], o_)\
                    .then_inc(sem("oThi_ready"), 1)

            exps(0)
            for n in range(NCH):
                if n + 1 < NCH:
                    exps(n + 1)
                probs_T(n)
                if n:
                    attended_hi(n - 1)
            attended_hi(NCH - 1)
            hi_panels.upto(P_FFN + 2)
            split_hi(1)
            act.wait_ge(sem("rs_ready"), 2)
            for c in range(FCH + 1):
                if c < FCH:
                    up = P_FFN + (3 * c if c else 1)
                    hi_panels.upto(up + 2)
                    act.wait_ge(panel_used, up + 1)
                    for b in range(TB):
                        i = act.activation(sil[:, b * 256:b * 256 + 256], bank[b][:, 0:256], ACT.Silu, scale=rs[:, b:b + 1])
                    i.then_inc(sem("sil_ready"), 1)
                    hi_panels.upto(up + (3 if c else 2))
                    act.wait_ge(sem("hidT_psum"), c + 1)
                    act.copy(hhi[:, :], bank[2]).then_inc(sem("hhi_ready"), 1)
            hi_panels.upto(P_IN + 2)
            split_hi(2)
            act.wait_ge(sem("rs_ready"), 3)
            act.wait_ge(phase_b_params, 32)
            act.copy(hhi[:, 0:256], wba[:, :]).then_inc(sem("wba_hi"), 1)
            act.wait_ge(loads, 96)
            act.activation(alog, alog, ACT.Exp)
            act.wait_ge(sem("ba_ready"), 1)
            act.activation(beta.rearrange("p (b h) -> p b h", b=TB),
                           ba.rearrange("p (b n) -> p b n", b=TB)[:, :, 0:VH], ACT.Exp, scale=-1.0)\
                .then_inc(sem("gate_act"), 1)
            act.wait_ge(sem("gate_dve"), 1)
            link(act.activation(sb_, sb_, ACT.Exp, scale=-1.0))
            act.activation(sb_, sb_, ACT.Ln, bias=1.0).then_inc(sem("gate_act"), 1)

            def gate_sums():
                act.wait_ge(sem("gsum_psum"), 1)
                act.activation(egl, bank[5][:, 64:128], ACT.Exp)
                act.activation(egc, bank[5][:, 0:32], ACT.Exp)
                act.copy(gc, bank[5][:, 0:32]).then_inc(sem("gate_act"), 1)
                act.wait_ge(sem("gate_dve"), 3)
                act.activation(etail, etail, ACT.Exp).then_inc(sem("gate_act"), 1)

            def four(n):
                return bank[n].rearrange("p (n f) -> p n f", n=4)

            def projected(g, part):
                act.wait_ge(panel_used, P_IN + 6 * g + 2 * part + 2)
                if part == 2:
                    act.wait_ge(sem("ch_psum"), 2 * g + 2)
                for b in range(TB):
                    if part < 2:
                        i = act.activation((group_part(g), prj_v)[part][:, b, :], bank[6 + b], ACT.Copy, scale=rs[:, b:b + 1])
                    else:
                        i = act.activation(group_part(g)[:, b, :], bank[6 + b], ACT.Silu, scale=rs[:, b:b + 1])
                i.then_inc(sem(("prj_qk_ready", "prj_v_ready", "z_ready")[part]), 1)

            for part in range(2):
                hi_panels.upto(P_IN + 2 * part + 3)
                projected(0, part)
                hi_panels.upto(P_IN + 2 * part + 4)
                if part == 0:
                    gate_sums()
            for g in range(GROUPS):
                nxt = P_IN + 6 * (g + 1)
                more = g + 1 < GROUPS
                for t in range(8):
                    if t % 4 == 0:
                        act.wait_ge(sem("ch_psum"), 2 * g + t // 4 + 1)
                    act.activation(cvall[:, t, :], conv_src(t), ACT.Copy, scale=tap(g, t, 3)).then_inc(sem("tap_ready"), 1)
                projected(g, 2)
                hi_panels.upto(nxt + 2)
                act.wait_ge(sem("conv_ready"), 2 * g + 1)
                act.activation(cvall[:, 0:4, :], cvall[:, 0:4, :], ACT.Silu).then_inc(sem("convs_ready"), 1)
                act.wait_ge(sem("back_psum"), 2 * g + 1)
                for n in range(8):
                    i = act.activation(qkT[:, n, :], bank[4 + n // 4][:, n % 4 * P:(n % 4 + 1) * P], ACT.Square,
                                       accum_out=ss8[:, n:n + 1])
                i.then_inc(sem("sq_ready"), 1)
                for b in range(TB):
                    i = act.copy(qk[:, 4 * b:4 * b + 4, :], four(4 + b))
                i.then_inc(sem("qk_ready"), 1)
                act.wait_ge(sem("conv_ready"), 2 * g + 2)
                act.activation(cvall[:, 4:8, :], cvall[:, 4:8, :], ACT.Silu).then_inc(sem("convs_ready"), 1)
                if more:
                    projected(g + 1, 0)
                act.wait_ge(sem("dec_ready"), g + 1)
                act.activation(dA, dA, ACT.Exp, scale=-1.0)
                act.activation(dT, dT, ACT.Exp).then_inc(sem("decay_ready"), 1)
                act.wait_ge(sem("qkT_psum"), g + 1)
                for b in range(TB):
                    i = act.copy(qkT[:, 4 * b:4 * b + 4, :], four(b))
                i.then_inc(sem("qkT_ready"), 1)
                act.wait_ge(sem("qdT_psum"), g + 1)
                for b in range(TB):
                    i = act.copy(qdecT[:, 4 * b:4 * b + 4, :], four(4 + b))
                i.then_inc(sem("qdT_ready"), 1)
                for b in range(TB):
                    act.wait_ge(sem("TT0_psum"), 2 * g + b + 1)
                    act.copy(TT[:, 4 * b:4 * b + 4, :], four(b)).then_inc(sem("TT0_ready"), 1)
                if more:
                    hi_panels.upto(nxt + SPLIT_AFTER[0])
                for lv in range(1, 6):
                    u = g * 5 + lv - 1
                    for b in range(TB):
                        act.wait_ge(sem("P_psum"), 2 * u + b + 1)
                        act.copy(Pm[:, 4 * b:4 * b + 4, :], four(2 + b)).then_inc(sem("P_ready"), 1)
                    if lv < 5:
                        v_ = g * 4 + lv - 1
                        for b in range(TB):
                            act.wait_ge(sem("T_psum"), 2 * v_ + b + 1)
                            act.copy(T[:, 4 * b:4 * b + 4, :], four(b)).then_inc(sem("T_ready"), 1)
                    if more:
                        if lv == 2:
                            projected(g + 1, 1)
                        hi_panels.upto(nxt + SPLIT_AFTER[lv])
                act.wait_ge(sem("wT_psum"), g + 1)
                for b in range(TB):
                    i = act.copy(wT[:, 4 * b:4 * b + 4, :], four(4 + b))
                i.then_inc(sem("wT_ready"), 1)
                for n in range(NCH):
                    r0 = n % 2 * CHUNK
                    act.wait_ge(sem("v_psum"), g * NCH + n + 1)
                    act.copy(vnew[r0:r0 + CHUNK, :, :], bank[2][r0:r0 + CHUNK, :].rearrange("p (h d) -> p h d", h=GH))\
                        .then_inc(sem("v_ready"), 1)
                    if n % 2:
                        b = n // 2
                        act.wait_ge(sem("o_psum"), g * TB + b + 1)
                        if b:
                            act.wait_ge(sem("rs_ready"), 3 + 3 * g + 2)
                        for h in range(GH):
                            i = act.activation(osq[:, h * P:(h + 1) * P], bank[b][:, h * P:(h + 1) * P], ACT.Square,
                                               accum_out=ss8[:, h:h + 1])
                        i.then_inc(sem("sq_ready"), 1)
                        if more:
                            hi_panels.upto(nxt + 7 + b)
            hi_panels.upto(P_DNO + 2)
            for f in range(8):
                act.wait_ge(sem("on_psum"), f + 1)
                if f >= 4:
                    act.wait_ge(panel_used, P_DNO + f - 4 + 1)
                act.copy(xhi[:, (f % 4) * 512:(f % 4 + 1) * 512], bank[f % 4]).then_inc(sem("onhi_ready"), 1)
                hi_panels.upto(P_DNO + f + 2)
            hi_panels.upto(P_MOE - 1)
            act.wait_ge(sem("h_ready"), 1)
            act.copy(h2hi, H3).then_inc(sem("h2hi_ready"), 1)
            for j in range(4):
                act.wait_ge(sem("hT_psum"), 13 + j)
                act.copy(hTf[:, 2 * j:2 * j + 2, :], bank[j].rearrange("p (k t) -> p k t", k=2)).then_inc(sem("hTf_ready"), 1)
            act.wait_ge(sem("route_dve"), 1)
            act.activation(e2[:, 0:2], e2[:, 0:2], ACT.Exp).then_inc(sem("route_act"), 1)
            act.wait_ge(sem("npass_ready"), 1)
            passes = act.value_load(npass[0:1, 0:1], min_val=1, max_val=2)

            def ehi(it, local, more=0):
                n = P_MOE + local
                act.wait_ge(landed[n % RAW], it * (16 * EP // RAW) + more * 16 + 16 * (n // RAW + 1))
                act.wait_ge(panel_used, it * EP + more * 6 + (n - SPLIT + 1))
                act.copy(slot(whi, n, SPLIT), slot(raw, n, RAW)).then_inc(hi_ready, 1)

            def silu(it, local, more=0):
                act.wait_ge(panel_used, it * EP + more * 6 + (P_MOE + local + 1))
                act.activation(sil[:, :], bank[0], ACT.Silu).then_inc(sem("esil_ready"), 1)

            def hidden_hi(u):
                act.wait_ge(sem("ehT_psum"), u + 1)
                act.copy(hhi[:, :], bank[2]).then_inc(sem("ehhi_ready"), 1)

            def gathered_hi(done):
                for h in range(2):
                    act.wait_ge(sem("gath_psum"), done + (h + 1))
                    act.copy(xhi[:, h * 512:(h + 1) * 512], bank[6 + h]).then_inc(sem("gxhi_ready"), 1)

            def output_hi(it):
                act.wait_ge(panel_used, it * EP + P_MOE)
                for h in range(2):
                    i = act.copy(yhi[:, h * 512:(h + 1) * 512], bank[3 + h])
                i.then_inc(sem("yhi_ready"), 1)

            act.wait_ge(sem("zeroed"), 1)
            gathered_hi(0)
            with act.Fori(0, passes) as q:
                with act.Fori(0, NE) as e:
                    it = q * NE + e
                    for i in range(3):
                        ehi(it, i)
                    output_hi(it)
                    for i in range(3, 6):
                        ehi(it, i)
                    silu(it, 3)
                    hidden_hi(it * ECH)
                    act.wait_ge(sem("selT_psum"), it + 1)
                    act.copy(selT[:, :], bank[6][:, 0:256]).then_inc(sem("selT_ready"), 1)
                    for i in range(6, 10):
                        ehi(it, i)
                    silu(it, 7)
                    ehi(it, 10)
                    ehi(it, 11)
                    hidden_hi(it * ECH + 1)
                    with act.Fori(2, ECH - 1) as c:
                        for i in range(12, 16):
                            ehi(it, i, c - 2)
                        silu(it, 13, c - 2)
                        ehi(it, 16, c - 2)
                        ehi(it, 17, c - 2)
                        hidden_hi(it * ECH + c)
                    for i in range(36, 40):
                        ehi(it, i)
                    silu(it, 37)
                    ehi(it, 40)
                    gathered_hi(it * 2 + 2)
                    ehi(it, 41)
                    hidden_hi(it * ECH + (ECH - 1))
            output_hi(passes * NE)

        @block.vector
        def _(dve):
            chain = [0]

            def link(i):
                chain[0] += 1
                i.then_inc(sem("dve_chain"), 1)
                dve.wait_ge(sem("dve_chain"), chain[0])

            def lo(n, v):
                dve.wait_ge(hi_ready, v + 1)
                dve.tensor_tensor(slot(wlo, n, SPLIT), slot(raw, n, RAW), slot(whi, n, SPLIT).bitcast(F32),
                                  ALU.subtract).then_inc(lo_ready, 1)

            lo_panels = Split(lo)
            def norm(n, g_, h_):
                dve.wait_ge(gain_loaded, 16 * (n - 2))
                for b in range(TB):
                    i = dve.tensor_tensor_reduce(h_[:, b, :], X[:, b, :], X[:, b, :], 1.0, 0.0, ALU.mult, ALU.add,
                                                 ms[:, b:b + 1])
                i.then_inc(sem("ms_ready"), 1)
                dve.wait_ge(sem("rs_ready"), n + 1 + 3 * GROUPS)
                for b in range(TB):
                    i = dve.scalar_tensor_tensor(out=h_[:, b, :], in0=X[:, b, :], scalar=rs[:, b:b + 1], in1=g_,
                                                 op0=ALU.mult, op1=ALU.mult)
                i.then_inc(sem("h_ready"), 1)

            def split_lo(norm):
                for j in range(4):
                    dve.wait_ge(sem("xhi_ready"), 4 * norm + j + 1)
                    for k in range(2 * j, 2 * j + 2):
                        s_ = slice(k * SEQ, (k + 1) * SEQ)
                        i = dve.scalar_tensor_tensor(out=xlo[:, s_], in0=bank[j][:, k % 2 * SEQ:(k % 2 + 1) * SEQ],
                                                     scalar=gcol[:, norm * KT + k:norm * KT + k + 1],
                                                     in1=xhi[:, s_].bitcast(F32), op0=ALU.mult, op1=ALU.subtract)
                    i.then_inc(sem("xlo_ready"), 1)

            def add_y(used):
                dve.wait_ge(panel_used, used)
                for h in range(2):
                    for b in range(TB):
                        s_ = X[:, b, h * 512:(h + 1) * 512]
                        i = dve.tensor_tensor(s_, s_, bank[4 + 2 * b + h], ALU.add)
                    i.then_inc(sem("x_ready"), 1)

            dve.memset(kT[:, :, 0:CHUNK], 0.0)
            dve.memset(vsh[0:HD, 0, :], 0.0).then_inc(sem("pads_ready"), 1)
            dve.wait_ge(sem("rows_psum"), 1)
            dve.tensor_copy(convw, bank[4][:, 4 * KT:4 * KT + P])
            dve.tensor_copy(gcol, bank[4][:, 0:4 * KT]).then_inc(sem("gcol_ready"), 1)
            dve.wait_ge(sem("gcol_ready"), 1)
            split_lo(0)
            dve.wait_ge(loads, 96)
            sk2 = sink16.rearrange("p (j r) -> p r j", r=2)
            for r in range(2):
                i = dve.tensor_copy(sink8[r * HD:(r + 1) * HD, :], sk2[r * HD:(r + 1) * HD, r, :])
            link(i)
            for c in range(3):
                lo_panels.upto(min(2 * c + 3, P_WO - 1))
                dve.wait_ge(panel_used, 2 * c + 2)
                dve.wait_ge(sem("rs_ready"), 1)
                for b in range(TB):
                    i = dve.scalar_tensor_tensor(out=qkv[:, b, c * 512:(c + 1) * 512], in0=bank[4 + 2 * (c % 2) + b],
                                                 scalar=rs[:, b:b + 1], in1=bqkv[:, c * 512:(c + 1) * 512],
                                                 op0=ALU.mult, op1=ALU.add)
                i.then_inc(sem("qkv_ready"), 1)
            lo_panels.upto(P_WO + 2)
            def largest(n):
                m = n % 2
                dve.wait_ge(sem("score_psum"), n + 1)
                if n >= 2:
                    dve.wait_ge(sem("pT_psum"), n - 1)
                for h in range(2):
                    i = dve.scalar_tensor_tensor(out=sc[:, m, h * 512:(h + 1) * 512], in0=bank[4 + 2 * m + h],
                                                 scalar=HD ** -0.5, in1=abias[:, 1 if n else 0, h * 512:(h + 1) * 512],
                                                 op0=ALU.mult, op1=ALU.add)
                link(i)
                link(dve.tensor_reduce(mx[m], sc[:, m, :].rearrange("p (j k) -> p j k", j=PAIRS), AX_X, ALU.max))
                link(dve.tensor_tensor(mx[m], mx[m], sink8, ALU.max))
                dve.tensor_scalar(nm[m], mx[m], -1.0, None, ALU.mult)
                dve.tensor_tensor(es[m], sink8, mx[m], ALU.subtract).then_inc(sem("max_ready"), 1)

            def normalised(n):
                m = n % 2
                s3 = sc[:, m, :].rearrange("p (j k) -> p j k", j=PAIRS)
                dve.wait_ge(sem("exp_ready"), n + 1)
                link(dve.tensor_tensor(ssum[m], ssum[m], es[m], ALU.add))
                link(dve.reciprocal(rsum[m], ssum[m]))
                dve.tensor_tensor(s3, s3, rsum[m].unsqueeze(2).broadcast_to([P, PAIRS, P]), ALU.mult)\
                    .then_inc(sem("probs_ready"), 1)

            def attended_lo(n):
                dve.wait_ge(sem("oThi_ready"), n + 1)
                x3 = xlo[:, :].rearrange("p (j t) -> p j t", j=PAIRS)[:, :, n * CHUNK:(n + 1) * CHUNK]
                h3 = xhi[:, :].bitcast(F32).rearrange("p (j t) -> p j t", j=PAIRS)[:, :, n * CHUNK:(n + 1) * CHUNK]
                dve.tensor_tensor(x3, bank[2 + n % 2].rearrange("p (j t) -> p j t", j=PAIRS), h3, ALU.subtract)\
                    .then_inc(sem("oTlo_ready"), 1)

            largest(0)
            largest(1)
            for n in range(NCH):
                normalised(n)
                if n:
                    attended_lo(n - 1)
                if n + 2 < NCH:
                    largest(n + 2)
            attended_lo(NCH - 1)
            lo_panels.upto(P_FFN + 2)
            add_y(P_FFN)
            split_lo(1)
            for c in range(FCH + 1):
                if c < FCH:
                    up = P_FFN + (3 * c if c else 1)
                    lo_panels.upto(up + 2)
                    dve.wait_ge(sem("sil_ready"), c + 1)
                    for b in range(TB):
                        s_ = slice(b * 256, b * 256 + 256)
                        i = dve.scalar_tensor_tensor(out=hid[:, s_], in0=bank[b][:, 256:512], scalar=rs[:, b:b + 1],
                                                     in1=sil[:, s_], op0=ALU.mult, op1=ALU.mult)
                    i.then_inc(sem("hid_ready"), 1)
                    lo_panels.upto(up + (3 if c else 2))
                    dve.wait_ge(sem("hhi_ready"), c + 1)
                    dve.tensor_tensor(hlo[:, :], bank[2], hhi[:, :].bitcast(F32), ALU.subtract)\
                        .then_inc(sem("hlo_ready"), 1)
            lo_panels.upto(P_IN + 2)
            add_y(P_IN)
            split_lo(2)
            dve.wait_ge(sem("wba_hi"), 1)
            dve.tensor_tensor(hlo[:, 0:256], wba[:, :], hhi[:, 0:256].bitcast(F32), ALU.subtract).then_inc(sem("wba_lo"), 1)
            dve.wait_ge(sem("ba_psum"), 1)
            dve.wait_ge(sem("rs_ready"), 3)
            for b in range(TB):
                i = dve.tensor_scalar(ba[:, b * 32:(b + 1) * 32], bank[4][:, b * 32:(b + 1) * 32], rs[:, b:b + 1], None, ALU.mult)
            i.then_inc(sem("ba_ready"), 1)
            dve.wait_ge(sem("ba_ready"), 1)
            dve.wait_ge(sem("gate_act"), 1)
            a2 = ba.rearrange("p (b n) -> p b n", b=TB)[:, :, VH:]
            two = lambda t: t.rearrange("p (b h) -> p b h", b=TB)
            twice = lambda t: t.unsqueeze(1).broadcast_to([P, TB, VH])
            dve.tensor_scalar(beta, beta, 1.0, None, ALU.add)
            link(dve.tensor_tensor(two(sa), a2, twice(dtb), ALU.add))
            dve.reciprocal(beta, beta)
            link(dve.tensor_scalar(sb_, sa, -1.0, None, ALU.mult))
            dve.tensor_tensor(sb_, sa, sb_, ALU.max).then_inc(sem("gate_dve"), 1)
            dve.wait_ge(sem("gate_act"), 2)
            link(dve.scalar_tensor_tensor(out=sb_, in0=sa, scalar=0.0, in1=sb_, op0=ALU.max, op1=ALU.add))
            dve.scalar_tensor_tensor(out=two(g32), in0=two(sb_), scalar=-1.0, in1=twice(alog),
                                     op0=ALU.mult, op1=ALU.mult).then_inc(sem("gate_dve"), 1)
            lo_panels.upto(P_IN + 4)
            dve.wait_ge(sem("gate_act"), 3)
            dve.scalar_tensor_tensor(out=ebeta, in0=beta, scalar=-1.0, in1=egc, op0=ALU.mult, op1=ALU.mult)
            dve.tensor_tensor(etail, bank[5][:, 32:64], gc, ALU.subtract).then_inc(sem("gate_dve"), 1)
            dve.wait_ge(sem("gate_act"), 4)
            lo_panels.upto(P_IN + 6)
            for g in range(GROUPS):
                nxt = P_IN + 6 * (g + 1)
                more = g + 1 < GROUPS
                for half in range(2):
                    for w in (2, 1, 0):
                        s_ = 3 - w
                        for t in range(4 * half, 4 * half + 4):
                            if w == 2:
                                dve.wait_ge(sem("tap_ready"), 8 * g + t // 2 * 2 + 2)
                            i = dve.scalar_tensor_tensor(out=cvall[:, t, s_:], in0=conv_src(t)[:, 0:SEQ - s_],
                                                         scalar=tap(g, t, w), in1=cvall[:, t, s_:], op0=ALU.mult, op1=ALU.add)
                        if w:
                            link(i)
                    i.then_inc(sem("conv_ready"), 1)
                lo_panels.upto(nxt + 2)
                dve.wait_ge(sem("R_psum"), g + 1)
                for n in range(8):
                    b, h = divmod(n, GH)
                    col = gc[:, b * VH + g * GH + h:b * VH + g * GH + h + 1]
                    r_ = bank[b][:, h * P:(h + 1) * P]
                    dve.scalar_tensor_tensor(out=dA[:, n, :], in0=r_, scalar=col, in1=tb_("off_strict"),
                                             op0=ALU.subtract, op1=ALU.add)
                    i = dve.scalar_tensor_tensor(out=dT[:, n, :], in0=r_, scalar=col, in1=tb_("off_upper"),
                                                 op0=ALU.subtract, op1=ALU.subtract)
                i.then_inc(sem("dec_ready"), 1)
                dve.wait_ge(sem("back_psum"), 2 * g + 2)
                for b in range(TB):
                    be = beta[:, b * VH + g * GH:b * VH + g * GH + GH].unsqueeze(2).broadcast_to([P, GH, P])
                    i = dve.tensor_tensor(vb[:, 4 * b:4 * b + 4, :], bank[2 + b].rearrange("p (n f) -> p n f", n=4), be, ALU.mult)
                i.then_inc(sem("vb_ready"), 1)
                dve.wait_ge(sem("qk_ready"), g + 1)
                dve.wait_ge(sem("rs_ready"), 3 + 3 * g + 1)
                r3 = r8.rearrange("p (b n) -> p b n", b=TB)
                link(dve.tensor_scalar(r3[:, :, 0:2], r3[:, :, 0:2], BH ** -0.5, None, ALU.mult))
                dve.tensor_tensor(qk, qk, r8.unsqueeze(2).broadcast_to([P, 8, P]), ALU.mult).then_inc(sem("qkn_ready"), 1)
                dve.wait_ge(sem("decay_ready"), g + 1)
                dve.wait_ge(sem("kk_psum"), g + 1)
                for n in range(8):
                    b, h = divmod(n, GH)
                    kk = bank[2 + b].rearrange("p (k m f) -> p k m f", k=2, m=2)[:, h // 2]
                    dve.scalar_tensor_tensor(out=A[:, n, :], in0=kk[:, 1, :], scalar=beta[:, b * VH + g * GH + h:b * VH + g * GH + h + 1],
                                             in1=dA[:, n, :], op0=ALU.mult, op1=ALU.mult)
                    i = dve.tensor_tensor(attnT[:, n, :], kk[:, 0, :], dT[:, n, :], ALU.mult)
                i.then_inc(sem("A_ready"), 1)
                dve.wait_ge(sem("A_ready"), g + 1)
                link(dve.tensor_tensor(T, A, tb_("level0").unsqueeze(1).broadcast_to([P, 8, P]), ALU.mult))
                dve.tensor_tensor(T, ident.unsqueeze(1).broadcast_to([P, 8, P]), T, ALU.subtract).then_inc(sem("T0_ready"), 1)
                if more:
                    lo_panels.upto(nxt + SPLIT_AFTER[0])
                for lv in range(1, 6):
                    u = g * 5 + lv - 1
                    for b in range(TB):
                        dve.wait_ge(sem("dTT_psum"), 2 * u + b + 1)
                        t_ = TT[:, 4 * b:4 * b + 4, :]
                        dve.tensor_tensor(t_, t_, bank[4 + b].rearrange("p (n f) -> p n f", n=4), ALU.subtract)\
                            .then_inc(sem("TT_ready"), 1)
                    if more:
                        lo_panels.upto(nxt + SPLIT_AFTER[lv])
                for n in range(NCH):
                    b = n // 2
                    if n < NCH - 1:
                        dve.wait_ge(sem("s_psum"), g * (NCH - 1) + n + 1)
                        for h in range(GH):
                            ps = bank[3][:, h * P:(h + 1) * P]
                            if n == 0:
                                i = dve.tensor_copy(S[:, h, :], ps)
                            else:
                                col = (n % 2) * 2 * VH + (n // 2) * VH + g * GH + h
                                i = dve.scalar_tensor_tensor(out=S[:, h, :], in0=S[:, h, :], scalar=egl[:, col:col + 1],
                                                             in1=ps, op0=ALU.mult, op1=ALU.add)
                        i.then_inc(sem("S_ready"), 1)
                    if n % 2:
                        dve.wait_ge(sem("rs_ready"), 3 + 3 * g + 2 + b)
                        o3 = otmp[:, :].rearrange("p (h d) -> p h d", h=GH)
                        link(dve.tensor_tensor(o3, bank[b].rearrange("p (h d) -> p h d", h=GH),
                                               r8[:, 0:4].unsqueeze(2).broadcast_to([P, GH, BH]), ALU.mult))
                        z_ = oall[:, b, g * 512:(g + 1) * 512]
                        dve.wait_ge(sem("zg_ready"), g + 1)
                        dve.tensor_tensor(z_, z_, otmp[:, :], ALU.mult).then_inc(sem("o_done"), 1)
                        if more:
                            lo_panels.upto(nxt + 7 + b)
            lo_panels.upto(P_DNO + 2)
            for f in range(8):
                dve.wait_ge(sem("onhi_ready"), f + 1)
                s_ = slice((f % 4) * 512, (f % 4 + 1) * 512)
                dve.tensor_tensor(xlo[:, s_], bank[f % 4], xhi[:, s_].bitcast(F32), ALU.subtract).then_inc(sem("onlo_ready"), 1)
                lo_panels.upto(P_DNO + f + 2)
            lo_panels.upto(P_MOE - 1)
            add_y(P_MOE)
            dve.wait_ge(sem("x_ready"), 6)
            norm(3, gain3[:, :], H3)
            dve.wait_ge(sem("h2hi_ready"), 1)
            dve.tensor_tensor(h2lo, H3, h2hi.bitcast(F32), ALU.subtract).then_inc(sem("h2lo_ready"), 1)
            dve.wait_ge(sem("logit_psum"), 1)
            link(dve.tensor_copy(lg, bank[4][:, 0:TB * NE]))
            topu = topi.bitcast(U32)
            for b in range(TB):
                i = dve.max(top[:, b * NE:(b + 1) * NE], lg[:, b * NE:(b + 1) * NE])
            link(i)
            for b in range(TB):
                i = dve.max_index(topu[:, b * NE:(b + 1) * NE], top[:, b * NE:(b + 1) * NE], lg[:, b * NE:(b + 1) * NE])
            link(i)
            link(dve.tensor_copy(tmp8, topu))
            t3 = top.rearrange("p (b e) -> p b e", b=TB)
            i3 = tmp8.rearrange("p (b e) -> p b e", b=TB)
            dve.tensor_tensor(e2[:, 0:2], t3[:, :, 1], t3[:, :, 0], ALU.subtract).then_inc(sem("route_dve"), 1)
            for b in range(TB):
                dve.tensor_scalar(oh1[:, b * NE:(b + 1) * NE], tb_("iota")[:, 0:NE], i3[:, b, 0:1], None, ALU.is_equal)
                i = dve.tensor_scalar(oh2[:, b * NE:(b + 1) * NE], tb_("iota")[:, 0:NE], i3[:, b, 1:2], None, ALU.is_equal)
            link(i)
            dve.tensor_tensor(msk, oh1, oh2, ALU.add).then_inc(sem("route_dve"), 1)
            dve.wait_ge(sem("route_act"), 1)
            link(dve.tensor_scalar(gt[:, 0:2], e2[:, 0:2], 1.0, None, ALU.add))
            link(dve.reciprocal(gt[:, 0:2], gt[:, 0:2]))
            link(dve.tensor_tensor(gt[:, 2:4], gt[:, 0:2], e2[:, 0:2], ALU.mult))
            for b in range(TB):
                s_ = slice(b * NE, (b + 1) * NE)
                i = dve.tensor_scalar(cmb[:, b, 1:], oh1[:, s_], gt[:, b:b + 1], None, ALU.mult)
            link(i)
            for b in range(TB):
                s_ = slice(b * NE, (b + 1) * NE)
                i = dve.scalar_tensor_tensor(out=cmb[:, b, 1:], in0=oh2[:, s_], scalar=gt[:, 2 + b:3 + b], in1=cmb[:, b, 1:],
                                             op0=ALU.mult, op1=ALU.add)
            link(i)
            dve.tensor_copy(cmb[:, :, 0:1], cmb[:, :, NE:])
            dve.wait_ge(sem("rank_psum"), 1)
            by_block = lambda t: t.rearrange("p (b e) -> p b e", b=TB)
            link(dve.tensor_tensor(pos[:, :, 0:NE], by_block(bank[5][:, 0:TB * NE]), by_block(msk), ALU.mult))
            link(dve.tensor_scalar(pos[:, :, 0:NE], pos[:, :, 0:NE], -1.0, None, ALU.add))
            dve.tensor_scalar(pos[:, :, NE:], pos[:, :, 0:1], -float(P), None, ALU.add)
            link(dve.tensor_reduce(cnt, bank[5][:, 16:16 + NE], AX_X, ALU.max))
            link(dve.tensor_scalar(cnt, cnt, float(P) + 0.5, 1.0, ALU.is_gt, ALU.add))
            link(dve.tensor_copy(npass[:, :], cnt))
            dve.tensor_copy(gt[:, 0:1], gt[:, 0:1]).then_inc(sem("npass_ready"), 1)
            dve.tensor_copy(gt[:, 1:2], gt[:, 1:2]).then_inc(sem("acc_added"), 1)
            dve.wait_ge(sem("npass_ready"), 1)
            passes = dve.value_load(npass[0:1, 0:1], min_val=1, max_val=2)

            def elo(it, local, more=0):
                n = P_MOE + local
                dve.wait_ge(hi_ready, it * EP + more * 6 + (n + 1))
                dve.tensor_tensor(slot(wlo, n, SPLIT), slot(raw, n, RAW), slot(whi, n, SPLIT).bitcast(F32),
                                  ALU.subtract).then_inc(lo_ready, 1)

            def hidden(u):
                dve.wait_ge(sem("esil_ready"), u + 1)
                dve.tensor_tensor(hid[:, :], bank[1], sil[:, :], ALU.mult).then_inc(sem("ehid_ready"), 1)

            def hidden_lo(u):
                dve.wait_ge(sem("ehhi_ready"), u + 1)
                dve.tensor_tensor(hlo[:, :], bank[2], hhi[:, :].bitcast(F32), ALU.subtract).then_inc(sem("ehlo_ready"), 1)

            def select(e):
                for b in range(TB):
                    i = dve.tensor_scalar(sel[:, b, :], tb_("iota"), pos[:, b, bass.ds(e, 1)], None, ALU.is_equal)
                i.then_inc(sem("sel_ready"), 1)

            def gathered_lo(done):
                for h in range(2):
                    dve.wait_ge(sem("gxhi_ready"), done + (h + 1))
                    s_ = slice(h * 512, (h + 1) * 512)
                    dve.tensor_tensor(xlo[:, s_], bank[6 + h], xhi[:, s_].bitcast(F32), ALU.subtract)\
                        .then_inc(sem("gxlo_ready"), 1)

            def output_lo(it):
                dve.wait_ge(sem("yhi_ready"), it + 1)
                for h in range(2):
                    s_ = slice(h * 512, (h + 1) * 512)
                    i = dve.tensor_tensor(ylo[:, s_], bank[3 + h], yhi[:, s_].bitcast(F32), ALU.subtract)
                i.then_inc(sem("ylo_ready"), 1)

            def add_output(it, weight, k):
                b, h = divmod(k, 2)
                dve.wait_ge(sem("comb_psum"), it * 4 + (k + 1))
                dve.wait_ge(sem("acc_added"), it * 4 + 1)
                s_ = X[:, b, h * 512:(h + 1) * 512]
                dve.scalar_tensor_tensor(out=s_, in0=bank[5 + k % 3], scalar=weight(b), in1=s_,
                                         op0=ALU.mult, op1=ALU.add).then_inc(sem("acc_added"), 1)

            dve.memset(selT[:, :].bitcast(F32), 0.0).then_inc(sem("selT_ready"), 1)
            for h in range(2):
                i = dve.memset(bank[3 + h], 0.0)
            i.then_inc(sem("zeroed"), 1)
            select(0)
            gathered_lo(0)
            with dve.Fori(0, passes) as q:
                with dve.Fori(0, NE) as e:
                    it = q * NE + e
                    weight = lambda b: cmb[:, b, bass.ds(e, 1)]
                    for i in range(3):
                        elo(it, i)
                    output_lo(it)
                    for i in range(3, 6):
                        elo(it, i)
                    hidden(it * ECH)
                    for k in range(3):
                        add_output(it, weight, k)
                    hidden_lo(it * ECH)
                    add_output(it, weight, 3)
                    for i in range(6, 10):
                        elo(it, i)
                    hidden(it * ECH + 1)
                    elo(it, 10)
                    elo(it, 11)
                    hidden_lo(it * ECH + 1)
                    with dve.Fori(2, ECH - 1) as c:
                        for i in range(12, 16):
                            elo(it, i, c - 2)
                        hidden(it * ECH + c)
                        elo(it, 16, c - 2)
                        elo(it, 17, c - 2)
                        hidden_lo(it * ECH + c)
                    select(e + 1)
                    for i in range(36, 40):
                        elo(it, i)
                    hidden(it * ECH + (ECH - 1))
                    elo(it, 40)
                    gathered_lo(it * 2 + 2)
                    elo(it, 41)
                    hidden_lo(it * ECH + (ECH - 1))
                dve.tensor_scalar(pos, pos, -float(P), None, ALU.add).then_inc(sem("pos_moved"), 1)
                dve.wait_ge(sem("pos_moved"), q + 1)
            turns = passes * NE
            output_lo(turns)
            for k in range(4):
                add_output(turns, lambda b: cmb[:, b, 0:1], k)
            dve.wait_ge(sem("acc_added"), turns * 4 + 5)
            norm(4, gain3[:, :], H3)

        @block.tensor
        def _(pe):
            def triple(ps, lhs_hi, lhs_lo, n, cols, start, stop):
                wh, wl = slot(whi, n, SPLIT)[:, cols], slot(wlo, n, SPLIT)[:, cols]
                pe.matmul(ps, lhs_hi, wh, start=start, stop=False)
                pe.matmul(ps, lhs_hi, wl, start=False, stop=False)
                return pe.matmul(ps, lhs_lo, wh, start=False, stop=stop)

            def xT(k, b):
                s_ = slice(k * SEQ + b * P, k * SEQ + (b + 1) * P)
                return xhi[:, s_], xlo[:, s_]

            def use(n):
                pe.wait_ge(lo_ready, n + 1)

            def wide_panels(n, outs):
                for half in range(2):
                    use(n + half)
                    for b in range(TB):
                        for k in range(4):
                            kt = half * 4 + k
                            i = triple(outs[b], *xT(kt, b), n + half, slice(k * 512, (k + 1) * 512), kt == 0, kt == KT - 1)
                    i.then_inc(panel_used, 1)
                return n + 2

            def narrow_panel(n, outs):
                use(n)
                for b in range(TB):
                    for k in range(KT):
                        i = triple(outs[b], *xT(k, b), n, slice(k * 256, (k + 1) * 256), k == 0, k == KT - 1)
                i.then_inc(panel_used, 1)
                return n + 1

            def row_panel(n, lhs, first, last):
                use(n)
                for b in range(TB):
                    for k in range(2):
                        for h in range(2):
                            i = triple(bank[4 + 2 * b + h], *lhs(k, b), n, slice(k * 1024 + h * 512, k * 1024 + (h + 1) * 512),
                                       first and k == 0, last and k == 1)
                i.then_inc(panel_used, 1)
                return n + 1

            def transposed(h_, norm):
                for j in range(4):
                    if norm == 0:
                        pe.wait_ge(x_loaded, 16)
                    elif norm < 3:
                        pe.wait_ge(sem("x_ready"), 2 * (norm - 1) + j // 2 + 1)
                    else:
                        pe.wait_ge(sem("h_ready"), 1)
                    for kk in range(2):
                        for b in range(TB):
                            k = 2 * j + kk
                            i = pe.transpose(bank[j][:, kk * SEQ + b * P:kk * SEQ + (b + 1) * P],
                                             h_[:, b, k * P:(k + 1) * P], ident)
                    i.then_inc(sem("hT_psum"), 1)

            pe.wait_ge(tab_loaded, 16)
            pe.wait_ge(sem("rows_loaded"), 32)
            pe.transpose(bank[4][:, 0:4 * KT], grow[:, :], ident[0:4 * KT, 0:4 * KT])
            pe.transpose(bank[4][:, 4 * KT:4 * KT + P], cwrow[:, :], ident).then_inc(sem("rows_psum"), 1)
            transposed(X, 0)
            pe.wait_ge(sem("xlo_ready"), 4)
            n = 0
            for c in range(3):
                if c == 2:
                    pe.wait_ge(sem("qkv_ready"), 1)
                n = wide_panels(n, [bank[4 + 2 * (c % 2) + b] for b in range(TB)])
            pe.wait_ge(sem("qkv_ready"), 3)
            for f in range(10):
                if f >= 4:
                    pe.wait_ge(sem("head_sb"), f - 3)
                for m in range(2):
                    col = (HEADS + 2 * f + m) * HD if f < 2 else (2 * f - 4 + m) * HD
                    for b in range(TB):
                        i = pe.transpose(bank[f % 4][0:HD, m * SEQ + b * P:m * SEQ + (b + 1) * P],
                                         qkv[:, b, col:col + HD], ident)
                i.then_inc(sem("head_psum"), 1)
            pe.wait_ge(sem("head_sb"), 10)
            pe.wait_ge(sem("pads_ready"), 1)

            def scores(n_):
                if n_ >= 2:
                    pe.wait_ge(sem("max_ready"), n_ - 1)
                for j in range(PAIRS):
                    o_ = bank[4 + 2 * (n_ % 2) + j // 4][:, j % 4 * P:(j % 4 + 1) * P]
                    i = pe.matmul(o_, qT[:, n_, 2 * j:2 * j + 2, :].rearrange("p h q -> p (h q)"),
                                  kT[:, j // 2, n_ * CHUNK:n_ * CHUNK + P], start=True, stop=True)
                i.then_inc(sem("score_psum"), 1)

            def probs_T(c):
                pe.wait_ge(sem("probs_ready"), c + 1)
                for j in range(PAIRS):
                    i = pe.transpose(bank[j // 4][:, j % 4 * P:(j % 4 + 1) * P], sc[:, c % 2, j * P:(j + 1) * P], ident)
                i.then_inc(sem("pT_psum"), 1)

            def attend(c):
                pe.wait_ge(sem("pT_ready"), c + 1)
                pe.wait_ge(sem("vsh_ready"), 1)
                if c >= 2:
                    pe.wait_ge(sem("oTlo_ready"), c - 1)
                for kv in range(KV_HEADS):
                    v_ = qkv[:, c // 2, QKV - 256 + kv * HD:QKV - 256 + (kv + 1) * HD] if c % 2 else \
                        vsh[:, c // 2, kv * HD:(kv + 1) * HD]
                    for r in range(2):
                        i = pe.matmul(bank[2 + c % 2][r * HD:(r + 1) * HD, kv * P:(kv + 1) * P], v_,
                                      pT[:, 2 * kv:2 * kv + 2, r * CHUNK:(r + 1) * CHUNK], start=True, stop=True)
                i.then_inc(sem("oT_psum"), 1)

            scores(0)
            scores(1)
            for c in range(NCH):
                probs_T(c)
                if c + 2 < NCH:
                    scores(c + 2)
                attend(c)
            pe.wait_ge(sem("oTlo_ready"), NCH)
            for c in range(4):
                n = row_panel(n, lambda k, b: xT(2 * c + k, b), c == 0, c == 3)
            transposed(X, 1)
            pe.wait_ge(sem("xlo_ready"), 8)

            def hT(k, b):
                s_ = slice(k * SEQ + b * P, k * SEQ + (b + 1) * P)
                return hhi[:, s_], hlo[:, s_]

            for c in range(FCH + 1):
                if c < FCH:
                    n = narrow_panel(n, [bank[b][:, 0:256] for b in range(TB)])
                    n = narrow_panel(n, [bank[b][:, 256:512] for b in range(TB)])
                if c:
                    pe.wait_ge(sem("hlo_ready"), c)
                    n = row_panel(n, hT, c == 1, c == FCH)
                if c < FCH:
                    pe.wait_ge(sem("hid_ready"), c + 1)
                    for k in range(2):
                        for b in range(TB):
                            i = pe.transpose(bank[2][:, k * SEQ + b * P:k * SEQ + (b + 1) * P],
                                             hid[:, b * 256 + k * P:b * 256 + (k + 1) * P], ident)
                    i.then_inc(sem("hidT_psum"), 1)
            transposed(X, 2)
            pe.wait_ge(sem("xlo_ready"), 12)
            pe.wait_ge(sem("wba_lo"), 1)
            for b in range(TB):
                o_ = bank[4][:, b * 32:(b + 1) * 32]
                for k in range(KT):
                    a_, l_ = xT(k, b)
                    s_ = slice(k * 32, (k + 1) * 32)
                    pe.matmul(o_, a_, hhi[:, s_], start=k == 0, stop=False)
                    pe.matmul(o_, a_, hlo[:, s_], start=False, stop=False)
                    i = pe.matmul(o_, l_, hhi[:, s_], start=False, stop=k == KT - 1)
            i.then_inc(sem("ba_psum"), 1)

            def gate_sums():
                pe.wait_ge(sem("gate_dve"), 2)
                for m, name in enumerate(("cum", "chunk", "first", "second")):
                    i = pe.matmul(bank[5][:, m * 32:(m + 1) * 32], tb_(name), g32, start=True, stop=True)
                i.then_inc(sem("gsum_psum"), 1)
            def project(g, i):
                m, b = divmod(i, 2)
                nn = P_IN + 6 * g + m
                if i == 0 and g:
                    pe.wait_ge(sem("z_ready"), g)
                if i == 4:
                    pe.wait_ge(sem("prj_qk_ready"), g + 1)
                if i == 8:
                    pe.wait_ge(sem("prj_v_ready"), g + 1)
                if b == 0:
                    use(nn)
                if m < 2:
                    for k in range(KT):
                        i_ = triple(bank[6 + b][:, m * 256:(m + 1) * 256], *xT(k, b), nn, slice(k * 256, (k + 1) * 256),
                                    k == 0, k == KT - 1)
                else:
                    for k in range(4):
                        kt = m % 2 * 4 + k
                        i_ = triple(bank[6 + b], *xT(kt, b), nn, slice(k * 512, (k + 1) * 512), kt == 0, kt == KT - 1)
                if b == 1:
                    i_.then_inc(panel_used, 1)

            for i in range(12):
                project(0, i)
                if i == 3:
                    gate_sums()
            pe.wait_ge(sem("gate_act"), 4)
            for g in range(GROUPS):
                more = g + 1 < GROUPS
                for half in range(2):
                    pe.wait_ge(sem(("prj_qk_ready", "prj_v_ready")[half]), g + 1)
                    for t in range(4 * half, 4 * half + 4):
                        src = (group_part(g), prj_v)[half]
                        for b in range(TB):
                            i = pe.transpose(conv_src(t)[:, b * P:(b + 1) * P], src[:, b, t % 4 * P:(t % 4 + 1) * P], ident)
                    i.then_inc(sem("ch_psum"), 1)
                pe.wait_ge(sem("gm_ready"), g + 1)
                if g:
                    pe.wait_ge(sem("o_done"), TB * g)
                for b in range(TB):
                    i = pe.matmul(bank[b], tb_("ones"), gm[:, 4 * b:4 * b + 4, :], start=True, stop=True)
                i.then_inc(sem("R_psum"), 1)
                for half in range(2):
                    if more:
                        project(g + 1, 2 * half)
                        project(g + 1, 2 * half + 1)
                    pe.wait_ge(sem("convs_ready"), 2 * g + half + 1)
                    for t in range(4):
                        for b in range(TB):
                            i = pe.transpose(bank[4 - 2 * half + b][:, t * P:(t + 1) * P],
                                             cvall[:, half * 4 + t, b * P:(b + 1) * P], ident)
                    i.then_inc(sem("back_psum"), 1)
                if more:
                    project(g + 1, 4)
                pe.wait_ge(sem("qkn_ready"), g + 1)
                pe.wait_ge(sem("dec_ready"), g + 1)
                for b in range(TB):
                    for t in range(4):
                        i = pe.transpose(bank[b][:, t * P:(t + 1) * P], qk[:, 4 * b + t, :], ident)
                i.then_inc(sem("qkT_psum"), 1)
                if more:
                    project(g + 1, 5)
                pe.wait_ge(sem("qkT_ready"), g + 1)
                pe.wait_ge(sem("vb_ready"), g + 1)
                for b in range(TB):
                    for kh in range(2):
                        kq = qkT[:, 4 * b:4 * b + 4, :].rearrange("p (m k) f -> p k m f", m=2)[:, kh]
                        i = pe.matmul(bank[2 + b][:, kh * 256:(kh + 1) * 256], qkT[:, 4 * b + 2 + kh, :], kq,
                                      start=True, stop=True)
                i.then_inc(sem("kk_psum"), 1)
                pe.wait_ge(sem("scaled"), 3 * g + 1)
                for m in range(8):
                    i = pe.transpose(bank[4 + m // 4][:, m % 4 * P:(m % 4 + 1) * P], qdec[:, m, :], ident)
                i.then_inc(sem("qdT_psum"), 1)
                pe.wait_ge(sem("T0_ready"), g + 1)
                for b in range(TB):
                    for h in range(GH):
                        i = pe.transpose(bank[b][:, h * P:(h + 1) * P], T[:, 4 * b + h, :], ident)
                    i.then_inc(sem("TT0_psum"), 1)
                pe.wait_ge(sem("qdT_ready"), g + 1)
                for lv in range(1, 6):
                    u = g * 5 + lv - 1
                    o = off0 if lv % 2 else off1
                    pe.wait_ge(sem("off_ready"), u + 1)
                    for b in range(TB):
                        if lv == 1:
                            pe.wait_ge(sem("TT0_ready"), 2 * g + b + 1)
                        else:
                            pe.wait_ge(sem("TT_ready"), 2 * (u - 1) + b + 1)
                        for h in range(GH):
                            i = pe.matmul(bank[2 + b][:, h * P:(h + 1) * P], o[:, 4 * b + h, :], TT[:, 4 * b + h, :],
                                          start=True, stop=True)
                        i.then_inc(sem("P_psum"), 1)
                    if more:
                        project(g + 1, 5 + lv)
                    for b in range(TB):
                        pe.wait_ge(sem("P_ready"), 2 * u + b + 1)
                        if lv > 1:
                            pe.wait_ge(sem("T_ready"), 2 * (g * 4 + lv - 2) + b + 1)
                        for h in range(GH):
                            i = pe.matmul(bank[4 + b][:, h * P:(h + 1) * P], T[:, 4 * b + h, :], Pm[:, 4 * b + h, :],
                                          start=True, stop=True)
                        i.then_inc(sem("dTT_psum"), 1)
                    if lv < 5:
                        for b in range(TB):
                            pe.wait_ge(sem("TT_ready"), 2 * u + b + 1)
                            for h in range(GH):
                                i = pe.transpose(bank[b][:, h * P:(h + 1) * P], TT[:, 4 * b + h, :], ident)
                            i.then_inc(sem("T_psum"), 1)
                pe.wait_ge(sem("TT_ready"), 2 * (g * 5 + 5))
                pe.wait_ge(sem("scaled"), 3 * g + 3)
                pe.wait_ge(sem("vb_ready"), g + 1)
                for m in range(8):
                    i = pe.matmul(bank[4 + m // 4][:, m % 4 * P:(m % 4 + 1) * P], kbe[:, m, :], TT[:, m, :], start=True, stop=True)
                i.then_inc(sem("wT_psum"), 1)
                for c in range(NCH):
                    b, r0 = c // 2, c % 2 * CHUNK
                    rr = slice(r0, r0 + CHUNK)
                    if c == 0:
                        pe.wait_ge(sem("wT_ready"), g + 1)
                    else:
                        pe.wait_ge(sem("S_ready"), g * (NCH - 1) + c)
                    for h in range(GH):
                        o_ = bank[2][rr, h * P:(h + 1) * P]
                        m = 4 * b + h
                        i = pe.matmul(o_, TT[:, m, rr], vb[:, m, :], start=True, stop=c == 0)
                        if c:
                            i = pe.matmul(o_, wT[:, m, rr], S[:, h, :], start=False, stop=True)
                    i.then_inc(sem("v_psum"), 1)
                    if more and c == 0:
                        project(g + 1, 11)
                    pe.wait_ge(sem("v_ready"), g * NCH + c + 1)
                    for h in range(GH):
                        o_ = bank[b][rr, h * P:(h + 1) * P]
                        m = 4 * b + h
                        i = pe.matmul(o_, attnT[rr, m, rr], vnew[rr, h, :], start=True, stop=c == 0)
                        if c:
                            i = pe.matmul(o_, qdecT[:, m, rr], S[:, h, :], start=False, stop=True)
                    if c % 2:
                        i.then_inc(sem("o_psum"), 1)
                    if c < NCH - 1:
                        for h in range(GH):
                            i = pe.matmul(bank[3][:, h * P:(h + 1) * P], ktail[rr, 4 * b + h, :], vnew[rr, h, :],
                                          start=True, stop=True)
                        i.then_inc(sem("s_psum"), 1)
            pe.wait_ge(sem("o_done"), TB * GROUPS)
            for f in range(8 + 1):
                if f < 8:
                    if f >= 4:
                        pe.wait_ge(sem("onlo_ready"), f - 3)
                    for kk in range(2):
                        for b in range(TB):
                            k = 2 * f + kk
                            i = pe.transpose(bank[f % 4][:, kk * SEQ + b * P:kk * SEQ + (b + 1) * P],
                                             oall[:, b, k * P:(k + 1) * P], ident)
                    i.then_inc(sem("on_psum"), 1)
                if f:
                    pe.wait_ge(sem("onlo_ready"), f)
                    n = row_panel(n, lambda k, b: xT((2 * (f - 1) + k) % 8, b), f == 1, f == 8)
            transposed(H3, 3)
            pe.wait_ge(sem("hTf_ready"), 4)
            for b in range(TB):
                for k in range(KT):
                    i = pe.matmul(bank[4][:, b * NE:(b + 1) * NE], hTf[:, k, b * P:(b + 1) * P], wr[:, k * NE:(k + 1) * NE],
                                  start=k == 0, stop=k == KT - 1)
            i.then_inc(sem("logit_psum"), 1)
            pe.wait_ge(sem("route_dve"), 2)
            pe.matmul(bank[5][:, 0:NE], tb_("tri"), msk[:, 0:NE], start=True, stop=True)
            pe.matmul(bank[5][:, NE:2 * NE], tb_("ones"), msk[:, 0:NE], start=True, stop=False)
            pe.matmul(bank[5][:, NE:2 * NE], tb_("tri"), msk[:, NE:2 * NE], start=False, stop=True)
            pe.matmul(bank[5][:, 2 * NE:3 * NE], tb_("ones"), msk[:, 0:NE], start=True, stop=False)
            pe.matmul(bank[5][:, 2 * NE:3 * NE], tb_("ones"), msk[:, NE:2 * NE], start=False, stop=True)\
                .then_inc(sem("rank_psum"), 1)
            pe.wait_ge(sem("h2lo_ready"), 1)
            pe.wait_ge(sem("npass_ready"), 1)
            passes = pe.value_load(npass[0:1, 0:1], min_val=1, max_val=2)

            def gxT(k):
                return xhi[:, k * P:(k + 1) * P], xlo[:, k * P:(k + 1) * P]

            def gate_up(it, local, more, u):
                for m in range(4):
                    nn = P_MOE + local + m
                    pe.wait_ge(lo_ready, it * EP + more * 6 + (nn + 1))
                    for k in range(4):
                        kt = m % 2 * 4 + k
                        i = triple(bank[m // 2], *gxT(kt), nn, slice(k * 512, (k + 1) * 512), kt == 0, kt == KT - 1)
                    i.then_inc(panel_used, 1)

            def down(it, local, more, u, first, last):
                pe.wait_ge(sem("ehlo_ready"), u + 1)
                for m in range(2):
                    nn = P_MOE + local + m
                    pe.wait_ge(lo_ready, it * EP + more * 6 + (nn + 1))
                    for k in range(2):
                        s_ = slice((2 * m + k) * P, (2 * m + k + 1) * P)
                        for h in range(2):
                            i = triple(bank[3 + h], hhi[:, s_], hlo[:, s_], nn, slice(k * 1024 + h * 512, k * 1024 + (h + 1) * 512),
                                       first and m == 0 and k == 0, last and m == 1 and k == 1)
                    i.then_inc(panel_used, 1)

            def hidden_T(u):
                pe.wait_ge(sem("ehid_ready"), u + 1)
                for k in range(4):
                    i = pe.transpose(bank[2][:, k * P:(k + 1) * P], hid[:, k * P:(k + 1) * P], ident)
                i.then_inc(sem("ehT_psum"), 1)

            def gather(tokens):
                pe.wait_ge(sem("sel_ready"), tokens + 1)
                for h in range(2):
                    for k in range(4):
                        o_ = bank[6 + h][:, k * P:(k + 1) * P]
                        d_ = slice((4 * h + k) * P, (4 * h + k + 1) * P)
                        for b in range(TB):
                            pe.matmul(o_, h2hi[:, b, d_], sel[:, b, :], start=b == 0, stop=False)
                            i = pe.matmul(o_, h2lo[:, b, d_], sel[:, b, :], start=False, stop=b == TB - 1)
                    i.then_inc(sem("gath_psum"), 1)

            def scatter(k):
                b, h = divmod(k, 2)
                s_, t_ = slice(h * 512, (h + 1) * 512), selT[:, b * P:(b + 1) * P]
                pe.matmul(bank[5 + k % 3], t_, yhi[:, s_], start=True, stop=False)
                pe.matmul(bank[5 + k % 3], t_, ylo[:, s_], start=False, stop=True).then_inc(sem("comb_psum"), 1)

            pe.wait_ge(sem("zeroed"), 1)
            gather(0)
            with pe.Fori(0, passes) as q:
                with pe.Fori(0, NE) as e:
                    it = q * NE + e
                    u0 = it * ECH
                    pe.wait_ge(sem("gxlo_ready"), it * 2 + 2)
                    gate_up(it, 0, 0, u0)
                    pe.wait_ge(sem("ylo_ready"), it + 1)
                    pe.wait_ge(sem("selT_ready"), it + 1)
                    for k in range(3):
                        scatter(k)
                    hidden_T(u0)
                    pe.wait_ge(sem("acc_added"), it * 4 + 2)
                    scatter(3)
                    pe.wait_ge(sem("acc_added"), it * 4 + 3)
                    for b in range(TB):
                        i = pe.transpose(bank[6][:, b * P:(b + 1) * P], sel[:, b, :].bitcast(F32), ident)
                    i.then_inc(sem("selT_psum"), 1)
                    gate_up(it, 4, 0, u0 + 1)
                    down(it, 8, 0, u0, True, False)
                    hidden_T(u0 + 1)
                    with pe.Fori(2, ECH - 1) as c:
                        gate_up(it, 10, c - 2, u0 + c)
                        down(it, 14, c - 2, u0 + (c - 1), False, False)
                        hidden_T(u0 + c)
                    gate_up(it, 34, 0, u0 + (ECH - 1))
                    pe.wait_ge(sem("acc_added"), it * 4 + 4)
                    pe.wait_ge(sem("selT_ready"), it + 2)
                    gather(it + 1)
                    down(it, 38, 0, u0 + (ECH - 2), False, False)
                    hidden_T(u0 + (ECH - 1))
                    down(it, EP - 2, 0, u0 + (ECH - 1), False, True)
            turns = passes * NE
            pe.wait_ge(sem("ylo_ready"), turns + 1)
            pe.wait_ge(sem("selT_ready"), turns + 1)
            pe.wait_ge(sem("gxlo_ready"), turns * 2 + 2)
            for k in range(4):
                if k == 3:
                    pe.wait_ge(sem("acc_added"), turns * 4 + 2)
                scatter(k)


_INS = ["x", "norm_g", "final_norm_g", "attn_w_qkv", "attn_b_qkv", "attn_sinks", "attn_w_o", "dn_w_in", "dn_conv_w",
        "dn_a_log", "dn_dt_bias", "dn_norm_g", "dn_w_o", "ffn_w_gate", "ffn_w_up", "ffn_w_down", "moe_w_router",
        "moe_w_gate", "moe_w_up", "moe_w_down"]
_SINGLE = ["attn_w_qkv", "attn_w_o", "dn_w_in", "dn_w_o", "ffn_w_gate", "ffn_w_up", "ffn_w_down",
           "moe_w_gate", "moe_w_up", "moe_w_down"]


def kernel(**inputs):
    import concourse.bacc as _bacc
    from concourse.bass_utils import run_bass_kernel_spmd as _run

    nc = _bacc.Bacc("TRN2", target_bir_lowering=False, num_devices=1)
    arrays, args = {}, []

    def given(name, a):
        arrays[name] = a
        return nc.dram_tensor(name, a.shape, mybir.dt.from_np(a.dtype), kind="ExternalInput").ap()

    for name in _INS:
        a = given(f"in_{name}_dram", np.ascontiguousarray(inputs[name]))
        args.append(a[0] if name in _SINGLE else a)
    args.append(given("table_dram", table()))
    args.append(given("alibi_dram", alibi()))
    args.append(nc.dram_tensor("out_0_dram", (1, SEQ, D), F32, kind="ExternalOutput").ap())
    trunk(nc, *args)
    r = _run(nc, [arrays], core_ids=[0])
    return r.results[0]["out_0_dram"]
```
